# Optimizing a Trainium2 kernel written in Bass

```python
import jax, jax.numpy as jnp
from jax import lax
import numpy as np

D_MODEL = 1024
BATCH = 1
SEQ = 1024
DEPTH = 1

CHUNK = 64
LEFT_CHUNKS = 8
BAND = LEFT_CHUNKS + 1
CONV_WIDTH = D_MODEL // 2
CONV_GROUP = 64
CONV_GROUPS = CONV_WIDTH // CONV_GROUP
CONV_K = 3
HEAD_DIM = 64
N_HEADS = (D_MODEL - CONV_WIDTH) // HEAD_DIM
ATTN_WIDTH = N_HEADS * HEAD_DIM
MIX_WIDTH = CONV_WIDTH + ATTN_WIDTH
IN_COLS = 3 * CONV_WIDTH + 3 * ATTN_WIDTH
REL_CLIP = 128
REL_TABLE = (CHUNK - 1) + REL_CLIP + 1
D_FF = 4 * D_MODEL
EPS = 1e-6
NEG_INF = -1e30

kernel_name = "hybrid_conv_chunkattn_block"

def rms_norm(x, g):
    xf = x.astype(jnp.float32)
    y = xf * lax.rsqrt(jnp.mean(xf * xf, axis=-1, keepdims=True) + EPS)
    return (y * g.astype(jnp.float32)).astype(x.dtype)

def group_rms_norm(y, g, group):
    shp = y.shape
    yf = y.astype(jnp.float32).reshape(shp[:-1] + (shp[-1] // group, group))
    yf = yf * lax.rsqrt(jnp.mean(yf * yf, axis=-1, keepdims=True) + EPS)
    return (yf.reshape(shp) * g.astype(jnp.float32)).astype(y.dtype)

def short_gated_conv(b, c, h, w_conv, b_conv):
    u = c * h
    y = lax.conv_general_dilated(
        u, w_conv[:, None, :].astype(u.dtype),
        window_strides=(1,), padding=[(CONV_K - 1, 0)],
        dimension_numbers=("NWC", "WIO", "NWC"),
        feature_group_count=CONV_WIDTH)
    return b * (y + b_conv)

def chunk_band_attention(q, k, v, q_gain, k_gain, rel_bias):
    bsz, s, _ = q.shape
    n = s // CHUNK
    q = q.reshape(bsz, n, CHUNK, N_HEADS, HEAD_DIM)
    k = k.reshape(bsz, n, CHUNK, N_HEADS, HEAD_DIM)
    v = v.reshape(bsz, n, CHUNK, N_HEADS, HEAD_DIM)
    q = rms_norm(q, q_gain)
    k = rms_norm(k, k_gain)
    pad = ((0, 0), (LEFT_CHUNKS, 0), (0, 0), (0, 0), (0, 0))
    kp = jnp.pad(k, pad)
    vp = jnp.pad(v, pad)
    k_band = jnp.concatenate([kp[:, o:o + n] for o in range(BAND)], axis=2)
    v_band = jnp.concatenate([vp[:, o:o + n] for o in range(BAND)], axis=2)
    scores = jnp.einsum("bnqhd,bnkhd->bnhqk", q, k_band).astype(jnp.float32)
    scores = scores * (HEAD_DIM ** -0.5)
    q_idx = jnp.arange(CHUNK)[:, None] + LEFT_CHUNKS * CHUNK
    k_idx = jnp.arange(BAND * CHUNK)[None, :]
    dist = jnp.clip(q_idx - k_idx, -(CHUNK - 1), REL_CLIP) + (CHUNK - 1)
    bias = rel_bias[:, dist].astype(jnp.float32)
    scores = scores + bias[None, None]
    key_chunk = (jnp.arange(n)[:, None] - LEFT_CHUNKS
                 + (jnp.arange(BAND * CHUNK) // CHUNK)[None, :])
    valid = key_chunk >= 0
    scores = jnp.where(valid[None, :, None, None, :], scores, NEG_INF)
    p = jax.nn.softmax(scores, axis=-1).astype(v.dtype)
    o = jnp.einsum("bnhqk,bnkhd->bnqhd", p, v_band)
    return o.reshape(bsz, s, ATTN_WIDTH)

def setup_inputs(seed: int = 0) -> dict:
    key = jax.random.key(seed)
    ks = jax.random.split(key, 16)
    f32 = jnp.float32
    nrm = lambda k, shp, sc: jax.random.normal(k, shp, f32) * sc
    gain = lambda k, shp: 1.0 + 0.01 * jax.random.normal(k, shp, f32)
    return {
        "x": jax.random.normal(ks[0], (BATCH, SEQ, D_MODEL), f32),
        "norm_mix_g": gain(ks[1], (DEPTH, D_MODEL)),
        "w_in": nrm(ks[2], (DEPTH, D_MODEL, IN_COLS), D_MODEL ** -0.5),
        "conv_w": nrm(ks[3], (DEPTH, CONV_K, CONV_WIDTH), CONV_K ** -0.5),
        "conv_b": nrm(ks[4], (DEPTH, CONV_WIDTH), 0.01),
        "q_norm_g": gain(ks[5], (DEPTH, HEAD_DIM)),
        "k_norm_g": gain(ks[6], (DEPTH, HEAD_DIM)),
        "rel_bias": nrm(ks[7], (DEPTH, N_HEADS, REL_TABLE), 0.1),
        "conv_out_g": gain(ks[8], (DEPTH, CONV_WIDTH)),
        "attn_out_g": gain(ks[9], (DEPTH, ATTN_WIDTH)),
        "w_out": nrm(ks[10], (DEPTH, MIX_WIDTH, D_MODEL), MIX_WIDTH ** -0.5),
        "norm_mlp_g": gain(ks[11], (DEPTH, D_MODEL)),
        "w_mlp_in": nrm(ks[12], (DEPTH, D_MODEL, D_FF), D_MODEL ** -0.5),
        "w_mlp_out": nrm(ks[13], (DEPTH, D_FF, D_MODEL), D_FF ** -0.5),
    }

def reference(x, norm_mix_g, w_in, conv_w, conv_b, q_norm_g, k_norm_g, rel_bias,
              conv_out_g, attn_out_g, w_out, norm_mlp_g, w_mlp_in, w_mlp_out):
    c0 = CONV_WIDTH
    a0 = 3 * CONV_WIDTH
    for l in range(DEPTH):
        xn = rms_norm(x, norm_mix_g[l])
        z = jnp.einsum("bsd,dc->bsc", xn, w_in[l])
        gb = z[..., 0:c0]
        gc = z[..., c0:2 * c0]
        hh = z[..., 2 * c0:3 * c0]
        q = z[..., a0:a0 + ATTN_WIDTH]
        k = z[..., a0 + ATTN_WIDTH:a0 + 2 * ATTN_WIDTH]
        v = z[..., a0 + 2 * ATTN_WIDTH:a0 + 3 * ATTN_WIDTH]
        y_conv = short_gated_conv(gb, gc, hh, conv_w[l], conv_b[l])
        y_attn = chunk_band_attention(q, k, v, q_norm_g[l], k_norm_g[l], rel_bias[l])
        y_mix = jnp.concatenate(
            [group_rms_norm(y_conv, conv_out_g[l], CONV_GROUP),
             group_rms_norm(y_attn, attn_out_g[l], HEAD_DIM)], axis=-1)
        x = x + jnp.einsum("bsc,cd->bsd", y_mix, w_out[l])
        xn = rms_norm(x, norm_mlp_g[l])
        hid = jnp.square(jax.nn.relu(jnp.einsum("bsd,df->bsf", xn, w_mlp_in[l])))
        x = x + jnp.einsum("bsf,fd->bsd", hid, w_mlp_out[l])
    return x


_drawn_inputs = setup_inputs


def setup_inputs(seed=0):
    import zlib

    import numpy as np

    out = dict(_drawn_inputs(seed))
    spreads = {}
    factors = {'norm_mix_g': 3.826,
     'conv_b': 64.0,
     'q_norm_g': 8.0,
     'k_norm_g': 8.0,
     'conv_out_g': 58.037,
     'attn_out_g': 56.689,
     'norm_mlp_g': 36.648,
     'rel_bias': 5.814}
    for name, (base, spread) in spreads.items():
        noise = np.random.default_rng([zlib.crc32(name.encode()), seed]).standard_normal(out[name].shape)
        drawn = base * np.exp(spread * noise) if base else spread * noise
        out[name] = __import__('jax').numpy.asarray(drawn.astype(out[name].dtype))
    for name, factor in factors.items():
        out[name] = (out[name] * factor).astype(out[name].dtype)
    return out
```

```python
import concourse.bass as bass
from concourse import mybir
from contextlib import ExitStack

F32 = mybir.dt.float32
F32R = mybir.dt.float32r
ALU = mybir.AluOpType
ACT = mybir.ActivationFunctionType
AX = mybir.AxisListType

P = 128
SEQ = 1024
DM = 1024
FF = 4 * DM
CHUNK = 64
LEFT = 8
CW = DM // 2
HD = 64
NHEAD = CW // HD
NTAB = 192
CLIP = 128
EPS = 1e-6
NEG = -1e30

NT = SEQ // P
KD = DM // P
HALF = 512
NH2 = SEQ // HALF
NPAIR = CW // P
PAIR = P // HD
MAXB = LEFT * CHUNK // P + 1
BANDW = MAXB * P
UNITS = NT * PAIR
FT = 4
NFB = FF // (FT * P)
REVW = BANDW + P - 1
VARY = BANDW - 2 * P
SKEW = REVW - VARY
PASSES = ((0, 0), (0, 1), (1, 0))
HI, LO = 0, 1
CBASE = {"q": 3 * CW, "k": 4 * CW, "v": 5 * CW, "C": CW, "H": 2 * CW, "B": 0}
ORDER = ("q", "k", "v", "C", "H", "B")
NW = len(ORDER)
NSLOT = 3


def build(nc, x, norm_mix_g, w_in, conv_w, conv_b, q_norm_g, k_norm_g, rel_bias,
          conv_out_g, attn_out_g, w_out, norm_mlp_g, w_mlp_in, w_mlp_out, out):
    ctx = ExitStack()
    with ctx:
        BASE = 16512
        KB = 1024
        RA, RB, RC, RD, RE = (BASE + KB * o for o in (0, 64, 96, 128, 192))

        def plan(at):
            cur = [at]

            def put(name, shape, dt):
                size = 4
                for n in shape[1:]:
                    size *= n
                t = nc.alloc_sbuf_tensor_at(name, list(shape), dt, offset=cur[0])
                cur[0] += (size + 31) // 32 * 32
                return t
            return put, cur

        actT = nc.alloc_sbuf_tensor_at("actT", [P, 2, KD, SEQ], F32R, offset=RA)
        xin = nc.alloc_sbuf_tensor_at("xin", [P, NT, DM], F32, offset=RB)
        ymix = nc.alloc_sbuf_tensor_at("ymix", [P, NT, KD, P], F32, offset=RB)
        hid = nc.alloc_sbuf_tensor_at("hid", [P, 2, FT, SEQ], F32R, offset=RB)
        h = nc.alloc_sbuf_tensor_at("h", [P, NT, DM], F32, offset=RC)
        wo = nc.alloc_sbuf_tensor_at("wo", [P, 2, 2, KD, HALF], F32R, offset=RD)
        w1 = nc.alloc_sbuf_tensor_at("w1", [P, 2, 2, KD, P], F32R, offset=RD)
        put, _ = plan(RD + 16 * KB)
        relu = put("relu", [P, 2, HALF], F32)
        hsq = put("hsq", [P, 2, HALF], F32)
        w2 = nc.alloc_sbuf_tensor_at("w2", [P, 2, FT, DM], F32R, offset=RD + 32 * KB)
        put, top = plan(RC)
        wsl = put("wsl", [P, NSLOT, 2, KD, P], F32R)
        qT = put("qT", [P, 2, SEQ], F32R)
        kT = put("kT", [P, 2, SEQ], F32R)
        V = put("V", [P, 2, NT, P], F32R)
        bias = put("bias", [P, PAIR, BANDW], F32)
        zs = put("zs", [P, 2, HALF], F32)
        sq = put("sq", [P, 2, HALF], F32)
        sqh = put("sqh", [P, 2, HALF], F32R)
        sql = put("sql", [P, 2, HALF], F32R)
        cs = put("cs", [P, HALF], F32)
        ub = put("ub", [P, HALF + 2], F32)
        vT = put("vT", [P, SEQ], F32)
        prob = put("prob", [P, 2, BANDW], F32)
        pT = put("pT", [P, 2, BANDW], F32R)
        on = put("on", [P, 2, HALF], F32)
        osq = put("osq", [P, HALF], F32)
        assert top[0] <= RE
        xs = nc.alloc_sbuf_tensor_at("xs", [P, 2, DM], F32, offset=RD + 32 * KB)
        junk = nc.alloc_sbuf_tensor_at("junk", [P, DM], F32, offset=RD + 40 * KB)
        rb = nc.alloc_sbuf_tensor_at("rb", [NHEAD, NTAB], F32, offset=RD + 44 * KB)
        rev = nc.alloc_sbuf_tensor_at("rev", [NHEAD, REVW], F32, offset=RD + 45 * KB)
        put, top = plan(RE)
        raw = put("raw", [P, 2, KD * P], F32)
        gB = put("gB", [P, DM], F32)
        ident = put("ident", [P, P], F32)
        ones = put("ones", [P, P], F32R)
        prm_all = put("prm_all", [P, 6, NPAIR], F32)
        prm = put("prm", [P, 6], F32)
        gqk = put("gqk", [P, 2], F32)
        eps = put("eps", [P, 1], F32)
        ssx = put("ssx", [P, NT], F32)
        sdx = put("sdx", [P, NT], F32)
        rsx = put("rsx", [P, NT], F32)
        negm = put("negm", [P, UNITS], F32)
        esum = put("esum", [P, UNITS], F32)
        orl = put("orl", [P, 8], F32)
        oss = put("oss", [P, 8], F32)
        osd = put("osd", [P, 8], F32)
        ors = put("ors", [P, 8], F32)
        assert top[0] <= nc.sbuf_usable_end
        W0, W1_, W2_, CB, CG, AG = range(6)

        PJ = ctx.enter_context(nc.psum_tensor("PJ", [P, 2, HALF], F32))
        SC = ctx.enter_context(nc.psum_tensor("SC", [P, 2 * HALF], F32))
        PT = ctx.enter_context(nc.psum_tensor("PT", [P, 2 * HALF], F32))
        OB = ctx.enter_context(nc.psum_tensor("OB", [P, HALF], F32))
        SS = ctx.enter_context(nc.psum_tensor("SS", [P, HALF], F32))
        MM2BANK = [SC[:, 0:HALF], SC[:, HALF:2 * HALF], PT[:, 0:HALF], PT[:, HALF:2 * HALF], OB[:, :], SS[:, :]]

        revd = nc.dram_tensor("revd", [NHEAD, REVW], F32, kind="Internal").ap()
        skewd = nc.dram_tensor("skewd", [NHEAD, P, SKEW], F32, kind="Internal").ap()

        names = """
        x_in g_in prm_in rel_in rev_out skew_out bias_in x_again g_again out_written
        consts passed mask_set masks_ok prm_g rev_built
        ssx_done sdx_done rsx_done xs_done tr_done xhi_done xlo_done junk_done
        whi_done w_ready proj_done ones_done vt_done sc_done pt_done pv_done ot_done
        prm_ready halo_done sql_done rs_done zn_done qklo_done vlo_done u_done t1_done t2_done t3_done y_done
        sm_done ptlo_done rl_done osc_done osq_done oss_done ors_done on_done
        zs_done sq_done sqh_done hi_done vcopy_done cs_done vhi_done exp_done pthi_done ss_read osd_done
        wohi_done wo_ready ymhi_done ym_ready mix_done hadd_done
        mm1_done mm2_done relu_done hsq_done hhi_done hlo_done acc_done
        """.split()
        s = {n: ctx.enter_context(nc.semaphore(n)) for n in names}
        PRIMED = 3

        def wait_alone(eng, sem, value):
            eng.wait_ge(sem, value)
            eng.sem_inc(s["passed"], 1)

        x_in = [ctx.enter_context(nc.semaphore(f"x_in{i}")) for i in range(NT // 2)]
        raw_in = [ctx.enter_context(nc.semaphore(f"raw_in{i}")) for i in range(2)]
        xr_in = [ctx.enter_context(nc.semaphore(f"xr_in{i}")) for i in range(NT)]

        x_t = x[0].rearrange("(t p) d -> p t d", p=P)
        out_t = out[0].rearrange("(t p) d -> p t d", p=P)
        w_in_t = w_in[0].rearrange("(k p) c -> p k c", p=P)
        w1_t = w_mlp_in[0].rearrange("(k p) f -> p k f", p=P)
        raw_k = raw[:, :, :].rearrange("p r (k c) -> p r k c", c=P)

        N_B = NPAIR * NW
        RAW_B = N_B // 2
        RAW_C = RAW_B + KD // 2
        D_ORDER = (("w1", 0), ("w1", 1), ("w2", 0), ("w2", 1), ("w1", 2), ("w2", 2), ("w1", 3), ("w2", 3))
        ND = len(D_ORDER)

        block = ctx.enter_context(nc.Block())

        @block.sync
        def _(sp):
            def load_in(it, w, more=0):
                cols = bass.ds(it * P + (CBASE[ORDER[w]] + more * P), P)
                sp.dma_start(raw_k[:, w % 2], w_in_t[:, :, cols]).then_inc(raw_in[w % 2], 16)

            for i in range(NT // 2):
                sp.dma_start(xin[:, 2 * i:2 * i + 2, :], x_t[:, 2 * i:2 * i + 2, :]).then_inc(x_in[i], 16)
                if i == 0:
                    sp.dma_start(gB[:, :], bass.AP(norm_mix_g.tensor, 0, [[0, P], [1, DM]])).then_inc(s["g_in"], 16)
                if i == 1:
                    load_in(0, 0)
                    load_in(0, 1)
            with sp.Fori(1, NPAIR) as nxt:
                for w in range(2, NW + 2):
                    sp.wait_ge(s["w_ready"], nxt * NW + (w - 1 - NW))
                    load_in(nxt, w % NW, -1 if w < NW else 0)
            for w in range(2, NW):
                sp.wait_ge(s["w_ready"], (NPAIR - 1) * NW + w - 1)
                load_in(NPAIR - 1, w)
            for k in range(KD):
                if k < 2:
                    sp.wait_ge(s["w_ready"], N_B - 1 + k)
                else:
                    sp.wait_ge(s["wo_ready"], k - 1)
                sp.dma_start(raw[:, k % 2, :], w_out[0, k * P:(k + 1) * P, :]).then_inc(raw_in[k % 2], 16)
            sp.wait_ge(s["mix_done"], 1)
            sp.wait_ge(s["on_done"], 2 * NPAIR)
            sp.wait_ge(s["zn_done"], 6 * NPAIR)
            sp.wait_ge(s["ot_done"], 2 * NPAIR)
            for t in range(NT):
                sp.dma_start(h[:, t, :], x_t[:, t, :]).then_inc(xr_in[t], 16)
            sp.dma_start(gB[:, :], bass.AP(norm_mlp_g.tensor, 0, [[0, P], [1, DM]])).then_inc(s["g_again"], 16)

            def load_mlp(b, j, more=0):
                kind, f = D_ORDER[j]
                f += more * FT
                if kind == "w1":
                    sp.dma_start(raw_k[:, j % 2], w1_t[:, :, bass.ds(b * (FT * P) + f * P, P)]).then_inc(raw_in[j % 2], 16)
                else:
                    sp.dma_start(raw[:, j % 2, :], w_mlp_out[0, bass.ds(b * (FT * P) + f * P, P), :]).then_inc(raw_in[j % 2], 16)

            for j in range(2):
                sp.wait_ge(s["wo_ready"], KD - 1 + j)
                load_mlp(0, j)
            with sp.Fori(2, NFB + 1) as nxt:
                for j in range(2, ND + 2):
                    sp.wait_ge(s["w_ready"], nxt * ND + (N_B + j - 1 - 2 * ND))
                    load_mlp(nxt, j % ND, -2 if j < ND else -1)
            for j in range(2, ND):
                sp.wait_ge(s["w_ready"], N_B + (NFB - 1) * ND + j - 1)
                load_mlp(NFB - 1, j)
            for t in range(NT):
                sp.wait_ge(s["acc_done"], (NFB - 1) * 2 * NT + 2 * (t + 1))
                sp.dma_start(out_t[:, t, :], h[:, t, :]).then_inc(s["out_written"], 16)
            sp.wait_ge(s["out_written"], 16 * NT)

        @block.gpsimd
        def _(pool):
            nc.gpsimd.memset(ident[:, :], 0.0).then_inc(s["consts"], 1)
            pool.wait_ge(s["consts"], 1)
            nc.gpsimd.affine_select(out=ident[:, :], in_=ident[:, :], compare_op=ALU.not_equal, fill=1.0, base=0,
                                    pattern=[[-1, P]], channel_multiplier=1).then_inc(s["consts"], 1)

            with pool.Fori(0, NPAIR) as it:
                for w in range(NW):
                    sl = w % NSLOT
                    pool.wait_ge(raw_in[w % 2], it * (NW // 2 * 16) + 16 * (w // 2 + 1))
                    wait_alone(pool, s["proj_done"], it * 12 + (PRIMED + 2 * (w - 2) if w >= NSLOT else w + 1))
                    nc.gpsimd.tensor_copy(wsl[:, sl, HI], raw_k[:, w % 2]).then_inc(s["whi_done"], 1)
                    pool.wait_ge(s["whi_done"], it * NW + (w + 1))
                    nc.gpsimd.tensor_tensor(wsl[:, sl, LO], raw_k[:, w % 2], wsl[:, sl, HI].bitcast(F32),
                                            ALU.subtract).then_inc(s["w_ready"], 1)
            pool.wait_ge(s["proj_done"], PRIMED + 12 * NPAIR + 2 * NT - 1)
            with pool.Fori(0, NFB) as b:
                for j, (kind, f) in enumerate(D_ORDER):
                    pool.wait_ge(raw_in[j % 2], b * (ND // 2 * 16) + 16 * (RAW_C + j // 2 + 1))
                    if kind == "w1":
                        wait_alone(pool, s["mm1_done"], b * (2 * FT) + (PRIMED + 2 * f - 2))
                        hi, lo, src = w1[:, f % 2, HI], w1[:, f % 2, LO], raw_k[:, j % 2]
                    else:
                        wait_alone(pool, s["mm2_done"], b * (2 * NT) + 1)
                        hi, lo, src = w2[:, HI, f], w2[:, LO, f], raw[:, j % 2, :]
                    nc.gpsimd.tensor_copy(hi, src).then_inc(s["whi_done"], 1)
                    pool.wait_ge(s["whi_done"], b * ND + (N_B + j + 1))
                    nc.gpsimd.tensor_tensor(lo, src, hi.bitcast(F32), ALU.subtract).then_inc(s["w_ready"], 1)

        @block.scalar
        def _(act):
            act.sem_inc(s["ss_read"], 1)
            for j in range(3):
                act.dma_start(prm_all[:, j, :], conv_w[0, j].rearrange("(i p) -> p i", p=P), allow_slow_non_contiguous=True).then_inc(s["prm_in"], 16)
            for j, g in ((CB, conv_b), (CG, conv_out_g), (AG, attn_out_g)):
                act.dma_start(prm_all[:, j, :], g[0].rearrange("(i p) -> p i", p=P), allow_slow_non_contiguous=True).then_inc(s["prm_in"], 16)
            for i, g in enumerate((q_norm_g, k_norm_g)):
                for r in range(PAIR):
                    act.dma_start(gqk[r * HD:(r + 1) * HD, i:i + 1], g.rearrange("o d -> d o"), allow_slow_non_contiguous=True).then_inc(s["prm_in"], 16)
            act.dma_start(rb[:, :], rel_bias[0]).then_inc(s["rel_in"], 16)
            act.wait_ge(s["rev_built"], 3)
            act.dma_start(revd, rev[:, :]).then_inc(s["rev_out"], 16)

            act.wait_ge(s["consts"], 2)
            for i in range(NT // 2):
                act.wait_ge(x_in[i], 16)
                for t in (2 * i, 2 * i + 1):
                    if t:
                        act.wait_ge(s["ssx_done"], t)
                    act.activation(junk[:, :], xin[:, t, :], ACT.Square, accum_out=ssx[:, t:t + 1]).then_inc(s["ssx_done"], 1)
                act.wait_ge(s["ssx_done"], 2 * i + 2)
                act.wait_ge(s["masks_ok"], 3)
                act.activation(sdx[:, 2 * i:2 * i + 2], ssx[:, 2 * i:2 * i + 2], ACT.Sqrt, bias=eps[:, 0:1],
                               scale=1.0 / DM).then_inc(s["sdx_done"], 1)
                if i == 1:
                    act.wait_ge(s["rev_out"], 16)
                    act.dma_start(skewd, bass.AP(revd.tensor, VARY, [[REVW, NHEAD], [0, P], [1, SKEW]])).then_inc(s["skew_out"], 16)
            with act.Fori(0, NT // 2) as i:
                for r, bank in ((0, SC), (1, PT)):
                    act.wait_ge(s["tr_done"], i * 2 + (r + 1))
                    act.activation(actT[:, HI, :, bass.ds(i * (2 * P) + r * P, P)],
                                   bank[:, :].rearrange("p (k c) -> p k c", c=P), ACT.Copy).then_inc(s["xhi_done"], 1)

            act.wait_ge(s["skew_out"], 16)
            with act.Fori(0, NPAIR) as it:
                for lo, hi, c0 in ((0, HD, 0), (HD, P, CHUNK)):
                    c1 = BANDW - CHUNK if lo == 0 else BANDW
                    act.dma_start(bias[lo:hi, :, c0:VARY],
                                  bass.AP(revd.tensor, it * (PAIR * REVW), [[0, hi - lo], [REVW, PAIR], [1, VARY - c0]])
                                  ).then_inc(s["bias_in"], 16)
                    act.dma_start(bias[lo:hi, :, VARY:c1],
                                  bass.AP(skewd.tensor, it * (PAIR * P * SKEW) + lo * (SKEW - 1) + P - 1,
                                          [[SKEW - 1, hi - lo], [P * SKEW, PAIR], [1, c1 - VARY]])
                                  ).then_inc(s["bias_in"], 16)

                def squares(n, src):
                    act.activation(sq[:, n % 2], src, ACT.Square).then_inc(s["sq_done"], 1)
                    act.activation(sqh[:, n % 2], src, ACT.Square).then_inc(s["sqh_done"], 1)

                def take(n):
                    if n >= 2:
                        act.wait_ge(s["qklo_done"], it * 4 + (n - 1))
                    act.wait_ge(s["proj_done"], it * 12 + (PRIMED + n + 1))
                    act.activation(zs[:, n % 2], PJ[:, n % 2], ACT.Copy).then_inc(s["zs_done"], 1)
                    squares(n, PJ[:, n % 2])

                def deviation(n, order):
                    act.wait_ge(s["ones_done"], it * 6 + (n + 1))
                    act.activation(sq[:, n % 2], SS[:, :], ACT.Sqrt, bias=eps[:, 0:1], scale=1.0 / HD).then_inc(s["ss_read"], 1)

                def qk_hi(n):
                    act.wait_ge(s["zn_done"], it * 6 + (n + 1))
                    dst = (qT, kT)[n // 2]
                    act.activation(dst[:, HI, (n % 2) * HALF:(n % 2 + 1) * HALF], zs[:, n % 2], ACT.Copy).then_inc(s["hi_done"], 1)

                take(0)
                take(1)
                deviation(0, 0)
                qk_hi(0)
                for n in (2, 3):
                    take(n)
                    deviation(n - 1, n - 1)
                    qk_hi(n - 1)
                for n in range(2):
                    act.wait_ge(s["proj_done"], it * 12 + (PRIMED + 5 + n))
                    act.activation(vT[:, n * HALF:(n + 1) * HALF], PJ[:, n], ACT.Copy).then_inc(s["vcopy_done"], 1)
                    if n == 0:
                        deviation(3, 3)
                        qk_hi(3)

                def c_copy(n):
                    act.wait_ge(s["proj_done"], it * 12 + (PRIMED + 7 + 3 * n))
                    if n:
                        act.wait_ge(s["u_done"], it * 2 + 1)
                    act.activation(cs[:, :], PJ[:, n % 2], ACT.Copy).then_inc(s["cs_done"], 1)

                c_copy(0)
                act.wait_ge(s["vt_done"], it + 1)
                act.activation(V[:, HI], PT[:, :].rearrange("p (t c) -> p t c", c=P), ACT.Copy).then_inc(s["vhi_done"], 1)

                def exps(u):
                    L = P * min(u // 2 + 1, MAXB)
                    act.wait_ge(s["sm_done"], it * UNITS + (u + 1))
                    act.activation(prob[:, u % 2, 0:L], prob[:, u % 2, 0:L], ACT.Exp, bias=negm[:, u:u + 1], scale=-1.0,
                                   accum_out=esum[:, u:u + 1]).then_inc(s["exp_done"], 1)

                def pt_hi(u):
                    L = P * min(u // 2 + 1, MAXB)
                    act.wait_ge(s["pt_done"], it * UNITS + (u + 1))
                    act.activation(pT[:, HI, 0:L], PT[:, 0:L], ACT.Copy).then_inc(s["pthi_done"], 1)

                def o_dev(g):
                    act.wait_ge(s["oss_done"], it * 2 + (g + 1))
                    act.activation(osd[:, :], oss[:, :], ACT.Sqrt, bias=eps[:, 0:1], scale=1.0 / HD).then_inc(s["osd_done"], 1)

                def o_store(g):
                    act.wait_ge(s["ot_done"], it * 2 + (g + 1))
                    act.activation(ymix[:, 4 * g:4 * g + 4, bass.ds(it + NPAIR, 1), :].rearrange("p t o c -> p t (o c)"),
                                   SS[:, :].rearrange("p (t c) -> p t c", c=P), ACT.Copy,
                                   scale=prm[:, AG:AG + 1]).then_inc(s["ss_read"], 1)

                exps(0)
                for u in range(UNITS):
                    if u + 1 < UNITS:
                        exps(u + 1)
                    pt_hi(u)
                    if u == 8:
                        act.wait_ge(s["y_done"], it * 2 + 1)
                        squares(4, zs[:, 0])
                    if u == 9:
                        o_dev(0)
                    if u == 10:
                        deviation(4, 4)
                    if u == 11:
                        c_copy(1)
                    if u == 12:
                        o_store(0)
                act.wait_ge(s["y_done"], it * 2 + 2)
                squares(5, zs[:, 1])
                o_dev(1)
                deviation(5, 6)
                o_store(1)
            act.wait_ge(s["ss_read"], 1 + 8 * NPAIR)
            act.wait_ge(s["on_done"], 2 * NPAIR)
            act.wait_ge(s["zn_done"], 6 * NPAIR)
            act.wait_ge(s["ot_done"], 2 * NPAIR)
            act.activation(osd[:, 0:1], eps[:, 0:1], ACT.Copy).then_inc(s["mix_done"], 1)

            def ym_hi(t):
                act.activation(actT[:, HI, :, t * P:(t + 1) * P], ymix[:, t], ACT.Copy).then_inc(s["ymhi_done"], 1)

            ym_hi(0)
            for k in range(KD):
                act.wait_ge(raw_in[k % 2], 16 * (RAW_B + k // 2 + 1))
                act.activation(wo[:, :, HI, k, :], raw[:, k % 2, :].rearrange("p (a c) -> p a c", a=2), ACT.Copy
                               ).then_inc(s["wohi_done"], 1)
            ym_hi(1)

            def hn_hi(t):
                act.wait_ge(s["tr_done"], NT + t + 1)
                act.activation(actT[:, HI, :, t * P:(t + 1) * P],
                               (SC, PT)[t % 2][:, :].rearrange("p (k c) -> p k c", c=P), ACT.Copy).then_inc(s["xhi_done"], 1)

            for t in range(NT):
                act.wait_ge(s["hadd_done"], 2 * t + 2)
                act.wait_ge(s["ym_ready"], t + 1)
                act.activation(ymix[:, t].rearrange("p k c -> p (k c)"), h[:, t, :], ACT.Square,
                               accum_out=ssx[:, t:t + 1]).then_inc(s["ssx_done"], 1)
                act.wait_ge(s["ssx_done"], NT + t + 1)
                act.activation(sdx[:, t:t + 1], ssx[:, t:t + 1], ACT.Sqrt, bias=eps[:, 0:1],
                               scale=1.0 / DM).then_inc(s["sdx_done"], 1)
                if t + 2 < NT:
                    ym_hi(t + 2)
                if t >= 1:
                    hn_hi(t - 1)
            hn_hi(NT - 1)

            with act.Fori(0, NFB) as b:
                def h_relu(g):
                    act.wait_ge(s["mm1_done"], b * (2 * FT) + (PRIMED + g + 1))
                    act.activation(relu[:, g % 2], PJ[:, g % 2], ACT.Relu).then_inc(s["relu_done"], 1)

                def h_hi(g):
                    act.wait_ge(s["hsq_done"], b * (2 * FT) + (g + 1))
                    act.activation(hid[:, HI, g // 2, (g % 2) * HALF:(g % 2 + 1) * HALF], hsq[:, g % 2], ACT.Copy
                                   ).then_inc(s["hhi_done"], 1)

                for g in range(2 * FT):
                    h_relu(g)
                    h_hi(g)

        @block.vector
        def _(dve):
            V_ = nc.vector
            V_.memset(eps[:, :], EPS).then_inc(s["masks_ok"], 1)
            V_.memset(bias[0:HD, :, BANDW - CHUNK:BANDW], NEG).then_inc(s["masks_ok"], 1)
            V_.memset(bias[HD:P, :, 0:CHUNK], NEG).then_inc(s["masks_ok"], 1)
            V_.memset(ones[:, :].bitcast(F32), 0.0).then_inc(s["mask_set"], 1)
            dve.wait_ge(s["mask_set"], 1)
            V_.memset(ones[0:HD, 0:HD].bitcast(F32), 1.0).then_inc(s["mask_set"], 1)
            V_.memset(ones[HD:P, HD:P].bitcast(F32), 1.0).then_inc(s["mask_set"], 1)
            flat = BANDW - CLIP
            dve.wait_ge(s["rel_in"], 16)
            V_.tensor_copy(rev[:, 0:flat], rb[:, NTAB - 1:NTAB].broadcast_to([NHEAD, flat])).then_inc(s["rev_built"], 1)
            V_.tensor_copy(rev[:, flat:flat + NTAB - 1], rb[:, NTAB - 2::-1]).then_inc(s["rev_built"], 1)
            V_.tensor_copy(rev[:, flat + NTAB - 1:REVW],
                           rb[:, 0:1].broadcast_to([NHEAD, REVW - flat - NTAB + 1])).then_inc(s["rev_built"], 1)

            dve.wait_ge(s["g_in"], 16)
            with dve.Fori(0, NT // 2) as i:
                dve.wait_ge(s["sdx_done"], i + 1)
                V_.reciprocal(rsx[:, bass.ds(i * 2, 2)], sdx[:, bass.ds(i * 2, 2)]).then_inc(s["rsx_done"], 1)
                dve.wait_ge(s["rsx_done"], i + 1)
                for r in range(2):
                    t = i * 2 + r
                    V_.scalar_tensor_tensor(xs[:, r, :], xin[:, bass.ds(t, 1), :].rearrange("p o d -> p (o d)"),
                                            rsx[:, bass.ds(t, 1)], gB[:, :], ALU.mult, ALU.mult).then_inc(s["xs_done"], 1)
                for r, bank in ((0, SC), (1, PT)):
                    dve.wait_ge(s["xhi_done"], i * 2 + (r + 1))
                    cols = bass.ds(i * (2 * P) + r * P, P)
                    V_.tensor_tensor(actT[:, LO, :, cols], bank[:, :].rearrange("p (k c) -> p k c", c=P),
                                     actT[:, HI, :, cols].bitcast(F32), ALU.subtract).then_inc(s["xlo_done"], 1)
            dve.wait_ge(s["prm_in"], 16 * 10)
            V_.tensor_scalar(gqk[:, 0:1], gqk[:, 0:1], HD ** -0.5, None, ALU.mult).then_inc(s["prm_g"], 1)
            dve.wait_ge(s["prm_g"], 1)
            dve.wait_ge(s["masks_ok"], 3)

            with dve.Fori(0, NPAIR) as it:
                dve.wait_ge(s["ss_read"], it * 8 + 1)
                V_.tensor_copy(prm[:, :], prm_all[:, :, bass.ds(it, 1)].rearrange("p a o -> p (a o)")).then_inc(s["prm_ready"], 1)
                V_.memset(ub[:, 0:2], 0.0).then_inc(s["halo_done"], 1)

                def squares_lo(n):
                    dve.wait_ge(s["sqh_done"], it * 6 + (n + 1))
                    V_.tensor_tensor(sql[:, n % 2], sq[:, n % 2], sqh[:, n % 2].bitcast(F32), ALU.subtract
                                     ).then_inc(s["sql_done"], 1)

                def normalise(n, order, dst, gain):
                    dve.wait_ge(s["ss_read"], it * 8 + (order + 2))
                    V_.reciprocal(sq[:, n % 2], sq[:, n % 2]).then_inc(s["rs_done"], 1)
                    dve.wait_ge(s["rs_done"], it * 6 + (n + 1))
                    V_.scalar_tensor_tensor(dst, zs[:, n % 2] if len(dst.shape) == 2 else zs[:, n % 2].rearrange("p (t c) -> p t c", c=P),
                                            gain,
                                            sq[:, n % 2] if len(dst.shape) == 2 else sq[:, n % 2].rearrange("p (t c) -> p t c", c=P),
                                            ALU.mult, ALU.mult).then_inc(s["zn_done"], 1)

                def qk_lo(n):
                    dst = (qT, kT)[n // 2]
                    c = slice((n % 2) * HALF, (n % 2 + 1) * HALF)
                    dve.wait_ge(s["hi_done"], it * 4 + (n + 1))
                    V_.tensor_tensor(dst[:, LO, c], zs[:, n % 2], dst[:, HI, c].bitcast(F32), ALU.subtract
                                     ).then_inc(s["qklo_done"], 1)

                squares_lo(0)
                squares_lo(1)
                for n in range(4):
                    normalise(n, n, zs[:, n % 2], gqk[:, n // 2:n // 2 + 1])
                    qk_lo(n)
                    if n < 2:
                        squares_lo(n + 2)
                dve.wait_ge(s["vhi_done"], it + 1)
                V_.tensor_tensor(V[:, LO], PT[:, :].rearrange("p (t c) -> p t c", c=P), V[:, HI].bitcast(F32),
                                 ALU.subtract).then_inc(s["vlo_done"], 1)

                def conv_gate(n):
                    dve.wait_ge(s["proj_done"], it * 12 + (PRIMED + 8 + 3 * n))
                    dve.wait_ge(s["cs_done"], it * 2 + (n + 1))
                    dve.wait_ge(s["halo_done"], it * 2 + (n + 1))
                    V_.tensor_tensor(ub[:, 2:HALF + 2], PJ[:, (7 + 3 * n) % 2], cs[:, :], ALU.mult).then_inc(s["u_done"], 1)

                def conv_taps(n):
                    z = zs[:, n]
                    dve.wait_ge(s["u_done"], it * 2 + (n + 1))
                    dve.wait_ge(s["prm_ready"], it + 1)
                    V_.tensor_scalar(z, ub[:, 2:HALF + 2], prm[:, W2_:W2_ + 1], prm[:, CB:CB + 1], ALU.mult, ALU.add
                                     ).then_inc(s["t1_done"], 1)
                    dve.wait_ge(s["t1_done"], it * 2 + (n + 1))
                    V_.scalar_tensor_tensor(z, ub[:, 1:HALF + 1], prm[:, W1_:W1_ + 1], z, ALU.mult, ALU.add
                                            ).then_inc(s["t2_done"], 1)
                    dve.wait_ge(s["t2_done"], it * 2 + (n + 1))
                    V_.scalar_tensor_tensor(z, ub[:, 0:HALF], prm[:, W0:W0 + 1], z, ALU.mult, ALU.add
                                            ).then_inc(s["t3_done"], 1)
                    dve.wait_ge(s["t3_done"], it * 2 + (n + 1))
                    if n == 0:
                        V_.tensor_copy(ub[:, 0:2], ub[:, HALF:HALF + 2]).then_inc(s["halo_done"], 1)

                def conv_out(n):
                    dve.wait_ge(s["proj_done"], it * 12 + (PRIMED + 9 + 3 * n))
                    V_.tensor_tensor(zs[:, n], PJ[:, (8 + 3 * n) % 2], zs[:, n], ALU.mult).then_inc(s["y_done"], 1)

                def conv_norm(n):
                    dst = ymix[:, 4 * n:4 * n + 4, bass.ds(it, 1), :].rearrange("p t o c -> p t (o c)")
                    normalise(4 + n, (4, 6)[n], dst, prm[:, CG:CG + 1])

                def scores(u):
                    L = P * min(u // 2 + 1, MAXB)
                    wait_alone(dve, s["sc_done"], it * UNITS + (u + 1))
                    V_.tensor_tensor_reduce(out=prob[:, u % 2, 0:L], in0=SC[:, 0:L], in1=bias[:, u % 2, BANDW - L:BANDW],
                                            scale=-1.0, scalar=3.0e38, op0=ALU.add, op1=ALU.min,
                                            accum_out=negm[:, u:u + 1]).then_inc(s["sm_done"], 1)

                def pt_lo(u):
                    L = P * min(u // 2 + 1, MAXB)
                    dve.wait_ge(s["pthi_done"], it * UNITS + (u + 1))
                    V_.tensor_tensor(pT[:, LO, 0:L], PT[:, 0:L], pT[:, HI, 0:L].bitcast(F32), ALU.subtract
                                     ).then_inc(s["ptlo_done"], 1)

                og = on[:, :, :].rearrange("p g (u d) -> p g u d", d=HD)

                def o_scale(g):
                    dve.wait_ge(s["exp_done"], it * UNITS + 8 * (g + 1))
                    V_.reciprocal(orl[:, :], esum[:, 8 * g:8 * g + 8]).then_inc(s["rl_done"], 1)
                    dve.wait_ge(s["rl_done"], it * 2 + (g + 1))
                    dve.wait_ge(s["pv_done"], it * UNITS + 8 * (g + 1))
                    V_.tensor_tensor(og[:, g], OB[:, :].rearrange("p (u d) -> p u d", d=HD),
                                     orl[:, :].rearrange("p (u o) -> p u o", o=1).broadcast_to([P, 8, HD]), ALU.mult
                                     ).then_inc(s["osc_done"], 1)
                    dve.wait_ge(s["osc_done"], it * 2 + (g + 1))
                    V_.tensor_tensor(osq[:, :], on[:, g], on[:, g], ALU.mult).then_inc(s["osq_done"], 1)
                    dve.wait_ge(s["osq_done"], it * 2 + (g + 1))
                    V_.tensor_reduce(oss[:, :], osq[:, :].rearrange("p (u d) -> p u d", d=HD), AX.X, ALU.add
                                     ).then_inc(s["oss_done"], 1)

                def o_norm(g):
                    dve.wait_ge(s["osd_done"], it * 2 + (g + 1))
                    V_.reciprocal(ors[:, :], osd[:, :]).then_inc(s["ors_done"], 1)
                    dve.wait_ge(s["ors_done"], it * 2 + (g + 1))
                    V_.tensor_tensor(og[:, g], og[:, g],
                                     ors[:, :].rearrange("p (u o) -> p u o", o=1).broadcast_to([P, 8, HD]), ALU.mult
                                     ).then_inc(s["on_done"], 1)

                dve.wait_ge(s["bias_in"], it * 64 + 64)
                scores(0)
                for u in range(UNITS):
                    if u + 1 < UNITS:
                        scores(u + 1)
                    pt_lo(u)
                    if u == 4:
                        conv_gate(0)
                        conv_taps(0)
                    if u == 7:
                        conv_out(0)
                    if u == 8:
                        o_scale(0)
                        squares_lo(4)
                    if u == 9:
                        o_norm(0)
                    if u == 11:
                        conv_norm(0)
                    if u == 14:
                        conv_gate(1)
                        conv_taps(1)
                conv_out(1)
                o_scale(1)
                squares_lo(5)
                conv_norm(1)
                o_norm(1)

            def ym_lo(t):
                dve.wait_ge(s["ymhi_done"], t + 1)
                V_.tensor_tensor(actT[:, LO, :, t * P:(t + 1) * P], ymix[:, t],
                                 actT[:, HI, :, t * P:(t + 1) * P].bitcast(F32), ALU.subtract).then_inc(s["ym_ready"], 1)

            ym_lo(0)
            for k in range(KD):
                dve.wait_ge(s["wohi_done"], k + 1)
                V_.tensor_tensor(wo[:, :, LO, k, :], raw[:, k % 2, :].rearrange("p (a c) -> p a c", a=2),
                                 wo[:, :, HI, k, :].bitcast(F32), ALU.subtract).then_inc(s["wo_ready"], 1)
            ym_lo(1)

            def hn_lo(t):
                dve.wait_ge(s["xhi_done"], NT + t + 1)
                V_.tensor_tensor(actT[:, LO, :, t * P:(t + 1) * P],
                                 (SC, PT)[t % 2][:, :].rearrange("p (k c) -> p k c", c=P),
                                 actT[:, HI, :, t * P:(t + 1) * P].bitcast(F32), ALU.subtract).then_inc(s["xlo_done"], 1)

            for t in range(NT):
                dve.wait_ge(xr_in[t], 16)
                for a in range(2):
                    c = slice(a * HALF, (a + 1) * HALF)
                    if t == NT - 1 and a == 1:
                        dve.wait_ge(s["mm2_done"], 1)
                    else:
                        dve.wait_ge(s["proj_done"], PRIMED + 12 * NPAIR + 2 * t + a + 1)
                    V_.tensor_tensor(h[:, t, c], PJ[:, a], h[:, t, c], ALU.add).then_inc(s["hadd_done"], 1)
                if t + 2 < NT:
                    ym_lo(t + 2)
                if t == 0:
                    dve.wait_ge(s["g_again"], 16)
                dve.wait_ge(s["sdx_done"], NT // 2 + t + 1)
                V_.reciprocal(rsx[:, t:t + 1], sdx[:, t:t + 1]).then_inc(s["rsx_done"], 1)
                dve.wait_ge(s["rsx_done"], NT // 2 + t + 1)
                V_.scalar_tensor_tensor(ymix[:, t].rearrange("p k c -> p (k c)"), h[:, t, :], rsx[:, t:t + 1], gB[:, :],
                                        ALU.mult, ALU.mult).then_inc(s["xs_done"], 1)
                if t >= 1:
                    hn_lo(t - 1)
            hn_lo(NT - 1)

            with dve.Fori(0, NFB) as b:
                def h_square(g):
                    dve.wait_ge(s["relu_done"], b * (2 * FT) + (g + 1))
                    V_.scalar_tensor_tensor(hsq[:, g % 2], PJ[:, g % 2], 0.0, relu[:, g % 2], ALU.max, ALU.mult
                                            ).then_inc(s["hsq_done"], 1)

                def h_lo(g):
                    dve.wait_ge(s["hhi_done"], b * (2 * FT) + (g + 1))
                    c = slice((g % 2) * HALF, (g % 2 + 1) * HALF)
                    V_.tensor_tensor(hid[:, LO, g // 2, c], hsq[:, g % 2], hid[:, HI, g // 2, c].bitcast(F32),
                                     ALU.subtract).then_inc(s["hlo_done"], 1)

                for g in range(2 * FT):
                    h_square(g)
                    h_lo(g)
                for m in range(2 * NT):
                    t, a = m // 2, m % 2
                    c = slice(a * HALF, (a + 1) * HALF)
                    dve.wait_ge(s["mm2_done"], b * (2 * NT) + (m + 2))
                    V_.tensor_tensor(h[:, t, c], MM2BANK[2 * (t % 3) + a], h[:, t, c], ALU.add).then_inc(s["acc_done"], 1)

        @block.tensor
        def _(pe):
            mm = nc.tensor.matmul
            pe.sem_inc(s["proj_done"], PRIMED)
            pe.sem_inc(s["mm1_done"], PRIMED)
            pe.wait_ge(s["consts"], 2)
            with pe.Fori(0, NT // 2) as i:
                for r, bank in ((0, SC), (1, PT)):
                    pe.wait_ge(s["xs_done"], i * 2 + (r + 1))
                    for k in range(KD):
                        last = nc.tensor.transpose(bank[:, k * P:(k + 1) * P], xs[:, r, k * P:(k + 1) * P], ident[:, :])
                    last.then_inc(s["tr_done"], 1)
            pe.wait_ge(s["xlo_done"], NT)
            pe.wait_ge(s["mask_set"], 3)

            with pe.Fori(0, NPAIR) as it:
                def proj_mm(g, w, half, r):
                    k, (a, b) = r // 3, PASSES[r % 3]
                    return mm(PJ[:, g % 2], wsl[:, w % NSLOT, a, k], actT[:, b, k, half * HALF:(half + 1) * HALF],
                              start=(r == 0), stop=(r == 3 * KD - 1))

                def project(g):
                    if g % 2 == 0:
                        pe.wait_ge(s["w_ready"], it * NW + (g // 2 + 1))
                    if g >= 2:
                        pe.wait_ge(s["sqh_done"], it * 6 + (g - 1))
                    for r in range(3 * KD):
                        last = proj_mm(g, g // 2, g % 2, r)
                    last.then_inc(s["proj_done"], 1)

                def sum_squares(n, order):
                    pe.wait_ge(s["sql_done"], it * 6 + (n + 1))
                    pe.wait_ge(s["ss_read"], it * 8 + (order + 1))
                    mm(SS[:, :], ones[:, :], sqh[:, n % 2], start=True, stop=False)
                    mm(SS[:, :], ones[:, :], sql[:, n % 2], start=False, stop=True).then_inc(s["ones_done"], 1)

                for g in range(6):
                    project(g)
                    if 1 <= g <= 4:
                        sum_squares(g - 1, g - 1)

                def conv_product(n):
                    q, r = n // (3 * KD), n % (3 * KD)
                    g, w, half = 6 + q, 3 + q % 3, q // 3
                    if r == 0:
                        if half == 0:
                            pe.wait_ge(s["w_ready"], it * NW + (w + 1))
                        sem, count = (("vcopy_done", 1), ("vcopy_done", 2), ("cs_done", 1),
                                      ("u_done", 1), ("y_done", 1), ("cs_done", 2))[q]
                        pe.wait_ge(s[sem], it * 2 + count)
                    last = proj_mm(g, w, half, r)
                    if r == 3 * KD - 1:
                        last.then_inc(s["proj_done"], 1)

                for n in range(3 * KD):
                    conv_product(n)
                pe.wait_ge(s["vcopy_done"], it * 2 + 2)
                for t in range(NT):
                    last = nc.tensor.transpose(PT[:, t * P:(t + 1) * P], vT[:, t * P:(t + 1) * P], ident[:, :])
                last.then_inc(s["vt_done"], 1)

                def score(u):
                    t, hh = u // 2, u % 2
                    nb = min(t + 1, MAXB)
                    hp = slice(hh * HD, (hh + 1) * HD)
                    if u == 0:
                        pe.wait_ge(s["qklo_done"], it * 4 + 4)
                    else:
                        pe.wait_ge(s["sm_done"], it * UNITS + u)
                    for c0 in range(0, nb * P, HALF):
                        c1 = min(c0 + HALF, nb * P)
                        k0 = (t - nb + 1) * P
                        for n, (a, b) in enumerate(PASSES):
                            last = mm(SC[:, c0:c1], qT[hp, a, t * P:(t + 1) * P], kT[hp, b, k0 + c0:k0 + c1],
                                      start=(n == 0), stop=(n == 2))
                    last.then_inc(s["sc_done"], 1)

                def prob_transpose(u):
                    nb = min(u // 2 + 1, MAXB)
                    pe.wait_ge(s["exp_done"], it * UNITS + (u + 1))
                    if u == 0:
                        pe.wait_ge(s["vlo_done"], it + 1)
                    else:
                        pe.wait_ge(s["ptlo_done"], it * UNITS + u)
                    for j in range(nb):
                        last = nc.tensor.transpose(PT[:, j * P:(j + 1) * P], prob[:, u % 2, j * P:(j + 1) * P], ident[:, :])
                    last.then_inc(s["pt_done"], 1)

                def prob_v(u):
                    t, hh = u // 2, u % 2
                    nb = min(t + 1, MAXB)
                    pe.wait_ge(s["ptlo_done"], it * UNITS + (u + 1))
                    if u == 8:
                        pe.wait_ge(s["osc_done"], it * 2 + 1)
                    o0 = (t % 4) * P + hh * HD
                    for j in range(nb):
                        for n, (a, b) in enumerate(PASSES):
                            last = mm(OB[:, o0:o0 + HD], pT[:, a, j * P:(j + 1) * P],
                                      V[:, b, t - nb + 1 + j, hh * HD:(hh + 1) * HD],
                                      start=(j == 0 and n == 0), stop=(j == nb - 1 and n == 2))
                    last.then_inc(s["pv_done"], 1)

                def o_transpose(g, order):
                    pe.wait_ge(s["on_done"], it * 2 + (g + 1))
                    pe.wait_ge(s["ss_read"], it * 8 + (order + 1))
                    for t in range(4):
                        last = nc.tensor.transpose(SS[:, t * P:(t + 1) * P], on[:, g, t * P:(t + 1) * P], ident[:, :])
                    last.then_inc(s["ot_done"], 1)

                n = 3 * KD
                score(0)
                for u in range(UNITS):
                    if u + 1 < UNITS:
                        score(u + 1)
                    for _ in range(4):
                        conv_product(n)
                        n += 1
                    if u >= 1:
                        prob_v(u - 1)
                    prob_transpose(u)
                    for _ in range(3):
                        conv_product(n)
                        n += 1
                    if u == 10:
                        sum_squares(4, 4)
                    if u == 12:
                        o_transpose(0, 5)
                while n < 6 * 3 * KD:
                    conv_product(n)
                    n += 1
                prob_v(UNITS - 1)
                sum_squares(5, 6)
                o_transpose(1, 7)

            def h_transpose(t):
                pe.wait_ge(s["xs_done"], NT + t + 1)
                if t >= 2:
                    pe.wait_ge(s["xlo_done"], NT + t - 1)
                bank = (SC, PT)[t % 2]
                for k in range(KD):
                    last = nc.tensor.transpose(bank[:, k * P:(k + 1) * P],
                                               ymix[:, t, k, :], ident[:, :])
                last.then_inc(s["tr_done"], 1)

            for t in range(NT):
                pe.wait_ge(s["ym_ready"], t + 1)
                for half in range(2):
                    if t:
                        pe.wait_ge(s["hadd_done"], 2 * t - 1 + half)
                    for k in range(KD):
                        if t == 0:
                            pe.wait_ge(s["wo_ready"], k + 1)
                        for n, (a, b) in enumerate(PASSES):
                            last = mm(PJ[:, half], actT[:, a, k, t * P:(t + 1) * P], wo[:, half, b, k, :],
                                      start=(k == 0 and n == 0), stop=(k == KD - 1 and n == 2))
                    last.then_inc(s["mm2_done" if t == NT - 1 and half else "proj_done"], 1)
                if t >= 1:
                    h_transpose(t - 1)
            h_transpose(NT - 1)

            pe.wait_ge(s["xlo_done"], 2 * NT)
            with pe.Fori(0, NFB) as b:
                for g in range(2 * FT):
                    f, half = g // 2, g % 2
                    if half == 0:
                        pe.wait_ge(s["w_ready"], b * ND + (N_B + D_ORDER.index(("w1", f)) + 1))
                    if g >= 2:
                        pe.wait_ge(s["hsq_done"], b * (2 * FT) + (g - 1))
                    for k in range(KD):
                        for n, (x0, x1) in enumerate(PASSES):
                            last = mm(PJ[:, half], w1[:, f % 2, x0, k], actT[:, x1, k, half * HALF:(half + 1) * HALF],
                                      start=(k == 0 and n == 0), stop=(k == KD - 1 and n == 2))
                    last.then_inc(s["mm1_done"], 1)

                def mm2(t, a, f):
                    for n, (x0, x1) in enumerate(PASSES):
                        last = mm(MM2BANK[2 * (t % 3) + a], hid[:, x0, f, t * P:(t + 1) * P],
                                  w2[:, x1, f, a * HALF:(a + 1) * HALF], start=(f == 0 and n == 0),
                                  stop=(f == FT - 1 and n == 2))
                    if f == FT - 1:
                        last.then_inc(s["mm2_done"], 1)

                pe.wait_ge(s["w_ready"], b * ND + (N_B + ND))
                for fs in (range(FT - 1), range(FT - 1, FT)):
                    pe.wait_ge(s["hlo_done"], b * (2 * FT) + 2 * (fs[-1] + 1))
                    for t in range(2):
                        for a in range(2):
                            for f in fs:
                                mm2(t, a, f)
                for t in range(2, NT):
                    for a in range(2):
                        if t >= 3:
                            pe.wait_ge(s["acc_done"], b * (2 * NT) + (2 * (t - 3) + a + 1))
                        for f in range(FT):
                            mm2(t, a, f)


_INS = ["x", "norm_mix_g", "w_in", "conv_w", "conv_b", "q_norm_g", "k_norm_g", "rel_bias",
        "conv_out_g", "attn_out_g", "w_out", "norm_mlp_g", "w_mlp_in", "w_mlp_out"]


def kernel(**inputs):
    import numpy as np
    import concourse.bacc as bacc
    from concourse.bass_utils import run_bass_kernel_spmd

    nc = bacc.Bacc("TRN2", target_bir_lowering=False, num_devices=1)
    arrays, args = {}, []
    for name in _INS:
        a = np.ascontiguousarray(inputs[name])
        arrays[f"in_{name}"] = a
        args.append(nc.dram_tensor(f"in_{name}", a.shape, mybir.dt.from_np(a.dtype), kind="ExternalInput").ap())
    args.append(nc.dram_tensor("out_0", (1, SEQ, DM), F32, kind="ExternalOutput").ap())
    build(nc, *args)
    r = run_bass_kernel_spmd(nc, [arrays], core_ids=[0])
    return r.results[0]["out_0"]
```

```python
import concourse.bass as bass
from concourse import mybir
from contextlib import ExitStack

F32 = mybir.dt.float32
F32R = mybir.dt.float32r
ALU = mybir.AluOpType
ACT = mybir.ActivationFunctionType
AX = mybir.AxisListType

P = 128
SEQ = 1024
DM = 1024
FF = 4 * DM
CHUNK = 64
LEFT = 8
CW = DM // 2
HD = 64
NHEAD = CW // HD
NTAB = 192
CLIP = 128
EPS = 1e-6
NEG = -1e30

NT = SEQ // P
KD = DM // P
HALF = 512
NH2 = SEQ // HALF
NPAIR = CW // P
PAIR = P // HD
MAXB = LEFT * CHUNK // P + 1
BANDW = MAXB * P
UNITS = NT * PAIR
FT = 4
NFB = FF // (FT * P)
REVW = BANDW + P - 1
VARY = BANDW - 2 * P
SKEW = REVW - VARY
PASSES = ((0, 0), (0, 1), (1, 0))
HI, LO = 0, 1
CBASE = {"q": 3 * CW, "k": 4 * CW, "v": 5 * CW, "C": CW, "H": 2 * CW, "B": 0}
ORDER = ("q", "k", "v", "C", "H", "B")
NW = len(ORDER)
NSLOT = 3


def build(nc, x, norm_mix_g, w_in, conv_w, conv_b, q_norm_g, k_norm_g, rel_bias,
          conv_out_g, attn_out_g, w_out, norm_mlp_g, w_mlp_in, w_mlp_out, out):
    ctx = ExitStack()
    with ctx:
        BASE = 16512
        KB = 1024
        RA, RB, RC, RD, RE = (BASE + KB * o for o in (0, 64, 96, 128, 192))

        def plan(at):
            cur = [at]

            def put(name, shape, dt):
                size = 4
                for n in shape[1:]:
                    size *= n
                t = nc.alloc_sbuf_tensor_at(name, list(shape), dt, offset=cur[0])
                cur[0] += (size + 31) // 32 * 32
                return t
            return put, cur

        actT = nc.alloc_sbuf_tensor_at("actT", [P, 2, KD, SEQ], F32R, offset=RA)
        xin = nc.alloc_sbuf_tensor_at("xin", [P, NT, DM], F32, offset=RB)
        ymix = nc.alloc_sbuf_tensor_at("ymix", [P, NT, KD, P], F32, offset=RB)
        put, top = plan(RB)
        w1 = put("w1", [P, 2, 2, KD, P], F32R)
        relu = put("relu", [P, 2, HALF], F32)
        hsq = put("hsq", [P, 2, HALF], F32)
        assert top[0] <= RC
        h = nc.alloc_sbuf_tensor_at("h", [P, NT, DM], F32, offset=RC)
        put, top = plan(RC)
        qT = put("qT", [P, 2, SEQ], F32R)
        zs = put("zs", [P, 3, HALF], F32)
        sq = put("sq", [P, 3, HALF], F32)
        cs = put("cs", [P, HALF], F32)
        ub = put("ub", [P, HALF + 2], F32)
        on = put("on", [P, 2, HALF], F32)
        osq = put("osq", [P, HALF], F32)
        assert top[0] <= RD
        wo = nc.alloc_sbuf_tensor_at("wo", [P, KD, 2, DM], F32R, offset=RD)
        hid = nc.alloc_sbuf_tensor_at("hid", [P, 2, FT, SEQ], F32R, offset=RD)
        w2 = nc.alloc_sbuf_tensor_at("w2", [P, 2, FT, DM], F32R, offset=RD + 32 * KB)
        put, top = plan(RD)
        wsl = put("wsl", [P, NSLOT, 2, KD, P], F32R)
        WO_EARLY = NSLOT
        kT = put("kT", [P, 2, SEQ], F32R)
        V = put("V", [P, 2, NT, P], F32R)
        bias = put("bias", [P, PAIR, BANDW], F32)
        prob = put("prob", [P, 2, BANDW], F32)
        pT = put("pT", [P, 2, BANDW], F32R)
        sqh = put("sqh", [P, 2, HALF], F32R)
        sql = put("sql", [P, 2, HALF], F32R)
        assert top[0] <= RE
        vT = nc.alloc_sbuf_tensor_at("vT", [P, SEQ], F32, offset=RD + 24 * KB + 16 * KB + 4 * PAIR * BANDW)
        woraw = nc.alloc_sbuf_tensor_at("woraw", [P, 2 * KD, SEQ], F32, offset=RA)
        junk = nc.alloc_sbuf_tensor_at("junk", [P, DM], F32, offset=RD + 52 * KB)
        rb = nc.alloc_sbuf_tensor_at("rb", [NHEAD, NTAB], F32, offset=RD + 57 * KB)
        rev = nc.alloc_sbuf_tensor_at("rev", [NHEAD, REVW], F32, offset=RD + 58 * KB)
        put, top = plan(RE)
        raw = put("raw", [P, 2, KD * P], F32)
        gB = put("gB", [P, DM], F32)
        ident = put("ident", [P, P], F32)
        ones = put("ones", [P, P], F32R)
        prm_all = put("prm_all", [P, 6, NPAIR], F32)
        prm = put("prm", [P, 6], F32)
        gqk = put("gqk", [P, 2], F32)
        eps = put("eps", [P, 1], F32)
        ssx = put("ssx", [P, NT], F32)
        sdx = put("sdx", [P, NT], F32)
        rsx = put("rsx", [P, NT], F32)
        negm = put("negm", [P, UNITS], F32)
        esum = put("esum", [P, UNITS], F32)
        orl = put("orl", [P, 8], F32)
        oss = put("oss", [P, 8], F32)
        osd = put("osd", [P, 8], F32)
        ors = put("ors", [P, 8], F32)
        assert top[0] <= nc.sbuf_usable_end

        def col(t):
            c = (t + NT // 2) % NT * P
            return slice(c, c + P)

        W0, W1_, W2_, CB, CG, AG = range(6)

        PJ = ctx.enter_context(nc.psum_tensor("PJ", [P, 2, HALF], F32))
        SC = ctx.enter_context(nc.psum_tensor("SC", [P, 2 * HALF], F32))
        PT = ctx.enter_context(nc.psum_tensor("PT", [P, 2 * HALF], F32))
        OB = ctx.enter_context(nc.psum_tensor("OB", [P, HALF], F32))
        SS = ctx.enter_context(nc.psum_tensor("SS", [P, HALF], F32))
        MM2BANK = [SC[:, 0:HALF], SC[:, HALF:2 * HALF], PT[:, 0:HALF], PT[:, HALF:2 * HALF], OB[:, :], SS[:, :]]

        revd = nc.dram_tensor("revd", [NHEAD, REVW], F32, kind="Internal").ap()
        skewd = nc.dram_tensor("skewd", [NHEAD, P, SKEW], F32, kind="Internal").ap()

        names = """
        x_in g_in prm_in rel_in rev_out skew_out bias_in x_again g_again out_written
        consts act_warm passed mask_set masks_ok prm_g rev_built
        ssx_done sdx_done rsx_done xs_done tr_done xhi_done xlo_done junk_done
        whi_done w_ready proj_done ones_done vt_done sc_done pt_done pv_done ot_done
        prm_ready halo_done sql_done rs_done zn_done qklo_done vlo_done u_done t1_done t2_done t3_done y_done
        sm_done ptlo_done rl_done osc_done osq_done oss_done ors_done on_done
        zs_done sq_done sqh_done hi_done vcopy_done cs_done vhi_done exp_done pthi_done ss_read osd_done
        wohi_done wo_ready ymhi_done ym_ready mix_done hadd_done
        mm1_done mm2_done relu_done hsq_done hhi_done hlo_done acc_done
        """.split()
        s = {n: ctx.enter_context(nc.semaphore(n)) for n in names}
        PRIMED = 3

        def wait_alone(eng, sem, value):
            eng.wait_ge(sem, value)
            eng.sem_inc(s["passed"], 1)

        x_in = [ctx.enter_context(nc.semaphore(f"x_in{i}")) for i in range(NT)]
        raw_in = [ctx.enter_context(nc.semaphore(f"raw_in{i}")) for i in range(2)]
        wor_in = [ctx.enter_context(nc.semaphore(f"wor_in{i}")) for i in range(KD)]
        xr_in = [ctx.enter_context(nc.semaphore(f"xr_in{i}")) for i in range(NT)]

        x_t = x[0].rearrange("(t p) d -> p t d", p=P)
        out_t = out[0].rearrange("(t p) d -> p t d", p=P)
        w_in_t = w_in[0].rearrange("(k p) c -> p k c", p=P)
        w1_t = w_mlp_in[0].rearrange("(k p) f -> p k f", p=P)
        raw_k = raw[:, :, :].rearrange("p r (k c) -> p r k c", c=P)

        N_B = NPAIR * NW
        RAW_B = N_B // 2
        G = 2 * NW
        D_ORDER = (("w1", 0), ("w1", 1), ("w2", 0), ("w2", 1), ("w1", 2), ("w2", 2), ("w1", 3), ("w2", 3))
        ND = len(D_ORDER)

        block = ctx.enter_context(nc.Block())

        @block.sync
        def _(sp):
            def load_in(it, w, more=0):
                cols = bass.ds(it * P + (CBASE[ORDER[w]] + more * P), P)
                sp.dma_start(raw_k[:, w % 2], w_in_t[:, :, cols]).then_inc(raw_in[w % 2], 16)

            for t in range(NT):
                sp.dma_start(xin[:, t, :], x_t[:, t, :]).then_inc(x_in[t], 16)
                if t == 0:
                    sp.dma_start(gB[:, :], bass.AP(norm_mix_g.tensor, 0, [[0, P], [1, DM]])).then_inc(s["g_in"], 16)
                if t in (1, 3):
                    load_in(0, t // 2)
            with sp.Fori(1, NPAIR) as nxt:
                for w in range(2, NW + 2):
                    sp.wait_ge(s["w_ready"], nxt * NW + (w - 1 - NW))
                    load_in(nxt, w % NW, -1 if w < NW else 0)
            for w in range(2, NW):
                sp.wait_ge(s["w_ready"], (NPAIR - 1) * NW + w - 1)
                load_in(NPAIR - 1, w)
            sp.wait_ge(s["proj_done"], PRIMED + (NPAIR - 1) * G + 9)
            for k in range(KD):
                sp.dma_start(woraw[:, 2 * k:2 * k + 2, 0:HALF],
                             w_out[0, k * P:(k + 1) * P, :].rearrange("p (a c) -> p a c", a=2)).then_inc(wor_in[k], 16)

            def load_mlp(b, j, more=0):
                kind, f = D_ORDER[j]
                f += more * FT
                if kind == "w1":
                    sp.dma_start(raw_k[:, j % 2], w1_t[:, :, bass.ds(b * (FT * P) + f * P, P)]).then_inc(raw_in[j % 2], 16)
                else:
                    sp.dma_start(raw[:, j % 2, :], w_mlp_out[0, bass.ds(b * (FT * P) + f * P, P), :]).then_inc(raw_in[j % 2], 16)

            for j in range(2):
                sp.wait_ge(s["w_ready"], N_B - 1 + j)
                load_mlp(0, j)
            sp.wait_ge(s["mix_done"], 1)
            for t in range(NT):
                sp.dma_start(h[:, t, :], x_t[:, t, :]).then_inc(xr_in[t], 16)
            sp.dma_start(gB[:, :], bass.AP(norm_mlp_g.tensor, 0, [[0, P], [1, DM]])).then_inc(s["g_again"], 16)
            with sp.Fori(2, NFB + 1) as nxt:
                for j in range(2, ND + 2):
                    sp.wait_ge(s["w_ready"], nxt * ND + (N_B + j - 1 - 2 * ND))
                    load_mlp(nxt, j % ND, -2 if j < ND else -1)
            for j in range(2, ND):
                sp.wait_ge(s["w_ready"], N_B + (NFB - 1) * ND + j - 1)
                load_mlp(NFB - 1, j)
            for t in range(NT):
                sp.wait_ge(s["acc_done"], (NFB - 1) * 2 * NT + 2 * (t + 1))
                sp.dma_start(out_t[:, t, :], h[:, t, :]).then_inc(s["out_written"], 16)
            sp.wait_ge(s["out_written"], 16 * NT)

        @block.gpsimd
        def _(pool):
            nc.gpsimd.memset(ident[:, :], 0.0).then_inc(s["consts"], 1)
            pool.wait_ge(s["consts"], 1)
            nc.gpsimd.affine_select(out=ident[:, :], in_=ident[:, :], compare_op=ALU.not_equal, fill=1.0, base=0,
                                    pattern=[[-1, P]], channel_multiplier=1).then_inc(s["consts"], 1)

            with pool.Fori(0, NPAIR) as it:
                for w in range(NW):
                    sl = w % NSLOT
                    pool.wait_ge(raw_in[w % 2], it * (NW // 2 * 16) + 16 * (w // 2 + 1))
                    wait_alone(pool, s["proj_done"], it * G + (PRIMED + (w + 1 if w >= NSLOT else w - 2)))
                    nc.gpsimd.tensor_copy(wsl[:, sl, HI], raw_k[:, w % 2]).then_inc(s["whi_done"], 1)
                    pool.wait_ge(s["whi_done"], it * NW + (w + 1))
                    nc.gpsimd.tensor_tensor(wsl[:, sl, LO], raw_k[:, w % 2], wsl[:, sl, HI].bitcast(F32),
                                            ALU.subtract).then_inc(s["w_ready"], 1)
            pool.wait_ge(s["tr_done"], NT + NT // 2)
            with pool.Fori(0, NFB) as b:
                for j, (kind, f) in enumerate(D_ORDER):
                    pool.wait_ge(raw_in[j % 2], b * (ND // 2 * 16) + 16 * (RAW_B + j // 2 + 1))
                    if kind == "w1":
                        wait_alone(pool, s["mm1_done"], b * (2 * FT) + (PRIMED + 2 * f - 2))
                        hi, lo, src = w1[:, f % 2, HI], w1[:, f % 2, LO], raw_k[:, j % 2]
                    else:
                        wait_alone(pool, s["mm2_done"], b * (2 * NT) + 1)
                        hi, lo, src = w2[:, HI, f], w2[:, LO, f], raw[:, j % 2, :]
                    nc.gpsimd.tensor_copy(hi, src).then_inc(s["whi_done"], 1)
                    pool.wait_ge(s["whi_done"], b * ND + (N_B + j + 1))
                    nc.gpsimd.tensor_tensor(lo, src, hi.bitcast(F32), ALU.subtract).then_inc(s["w_ready"], 1)

        GROUPS = (("q", 0), ("k", 0), ("v", 0), ("q", 1), ("k", 1), ("v", 1),
                  ("C", 0), ("H", 0), ("B", 0), ("C", 1), ("H", 1), ("B", 1))
        QKGROUP = (0, 1, 3, 4)
        SSORDER = (0, 1, 2, 3, 4, 6)

        def half(n):
            return slice(n * HALF, (n + 1) * HALF)

        def zbuf(n):
            return n % 2 if n < 4 else 2

        def keys(u):
            return min(u // 2 + 1, MAXB)

        @block.scalar
        def _(act):
            act.sem_inc(s["ss_read"], 1)
            act.dma_start(rb[:, :], rel_bias[0]).then_inc(s["rel_in"], 16)
            act.wait_ge(s["masks_ok"], 3)
            act.activation(osd[:, 0:1], eps[:, 0:1], ACT.Sqrt).then_inc(s["act_warm"], 1)

            def params_in():
                for i, g in enumerate((q_norm_g, k_norm_g)):
                    for r in range(PAIR):
                        act.dma_start(gqk[r * HD:(r + 1) * HD, i:i + 1], g.rearrange("o d -> d o"),
                                      allow_slow_non_contiguous=True).then_inc(s["prm_in"], 16)
                for j, g in ((W0, conv_w[0, 0]), (W1_, conv_w[0, 1]), (W2_, conv_w[0, 2]), (CB, conv_b[0]),
                             (CG, conv_out_g[0]), (AG, attn_out_g[0])):
                    act.dma_start(prm_all[:, j, :], g.rearrange("(i p) -> p i", p=P),
                                  allow_slow_non_contiguous=True).then_inc(s["prm_in"], 16)

            def x_stats(t):
                act.wait_ge(x_in[t], 16)
                if t:
                    act.wait_ge(s["ssx_done"], t)
                act.activation(junk[:, :], xin[:, t, :], ACT.Square, accum_out=ssx[:, t:t + 1]).then_inc(s["ssx_done"], 1)
                act.wait_ge(s["ssx_done"], t + 1)
                act.activation(sdx[:, t:t + 1], ssx[:, t:t + 1], ACT.Sqrt, bias=eps[:, 0:1],
                               scale=1.0 / DM).then_inc(s["sdx_done"], 1)

            def x_hi(t):
                act.wait_ge(s["tr_done"], t + 1)
                act.activation(actT[:, HI, :, t * P:(t + 1) * P],
                               (SC, PT)[t % 2][:, :].rearrange("p (k c) -> p k c", c=P), ACT.Copy).then_inc(s["xhi_done"], 1)

            for t in range(NT):
                x_stats(t)
                if t == 1:
                    params_in()
                if t == 3:
                    act.wait_ge(s["rev_built"], 3)
                    act.dma_start(revd, rev[:, :]).then_inc(s["rev_out"], 16)
                if t >= 2:
                    x_hi(t - 2)
            act.wait_ge(s["rev_out"], 16)
            act.dma_start(skewd, bass.AP(revd.tensor, VARY, [[REVW, NHEAD], [0, P], [1, SKEW]])).then_inc(s["skew_out"], 16)
            x_hi(NT - 2)
            x_hi(NT - 1)

            def squares(it, n, src):
                act.activation(sq[:, zbuf(n)], src, ACT.Square).then_inc(s["sq_done"], 1)
                act.activation(sqh[:, n % 2], src, ACT.Square).then_inc(s["sqh_done"], 1)

            def take(it, n):
                if n >= 2:
                    act.wait_ge(s["qklo_done"], it * 4 + (n - 1))
                g = QKGROUP[n]
                act.wait_ge(s["proj_done"], it * G + (PRIMED + g + 1))
                act.activation(zs[:, n % 2], PJ[:, g % 2], ACT.Copy).then_inc(s["zs_done"], 1)
                squares(it, n, PJ[:, g % 2])

            def deviation(it, n):
                act.wait_ge(s["ones_done"], it * 6 + (n + 1))
                act.activation(sq[:, zbuf(n)], SS[:, :], ACT.Sqrt, bias=eps[:, 0:1], scale=1.0 / HD).then_inc(s["ss_read"], 1)

            def qk_hi(it, n):
                act.wait_ge(s["zn_done"], it * 6 + (n + 1))
                act.activation((qT, kT)[n % 2][:, HI, half(n // 2)], zs[:, n % 2], ACT.Copy).then_inc(s["hi_done"], 1)

            def v_copy(it, n):
                g = 2 + 3 * n
                act.wait_ge(s["proj_done"], it * G + (PRIMED + g + 1))
                act.activation(vT[:, half(n)], PJ[:, g % 2], ACT.Copy).then_inc(s["vcopy_done"], 1)

            def c_copy(it, n):
                g = 6 + 3 * n
                act.wait_ge(s["proj_done"], it * G + (PRIMED + g + 1))
                if n:
                    act.wait_ge(s["u_done"], it * 2 + 1)
                act.activation(cs[:, :], PJ[:, g % 2], ACT.Copy).then_inc(s["cs_done"], 1)

            def exps(it, u):
                L = P * keys(u)
                act.wait_ge(s["sm_done"], it * UNITS + (u + 1))
                act.activation(prob[:, u % 2, 0:L], prob[:, u % 2, 0:L], ACT.Exp, bias=negm[:, u:u + 1], scale=-1.0,
                               accum_out=esum[:, u:u + 1]).then_inc(s["exp_done"], 1)

            def pt_hi(it, u):
                L = P * keys(u)
                act.wait_ge(s["pt_done"], it * UNITS + (u + 1))
                act.activation(pT[:, HI, 0:L], PT[:, 0:L], ACT.Copy).then_inc(s["pthi_done"], 1)

            def o_dev(it, g):
                act.wait_ge(s["oss_done"], it * 2 + (g + 1))
                act.activation(osd[:, :], oss[:, :], ACT.Sqrt, bias=eps[:, 0:1], scale=1.0 / HD).then_inc(s["osd_done"], 1)

            def o_store(it, g):
                act.wait_ge(s["ot_done"], it * 2 + (g + 1))
                act.activation(ymix[:, 4 * g:4 * g + 4, bass.ds(it + NPAIR, 1), :].rearrange("p t o c -> p t (o c)"),
                               SS[:, :].rearrange("p (t c) -> p t c", c=P), ACT.Copy,
                               scale=prm[:, AG:AG + 1]).then_inc(s["ss_read"], 1)

            def bias_load(it):
                for lo, hi, c0 in ((0, HD, 0), (HD, P, CHUNK)):
                    c1 = BANDW - CHUNK if lo == 0 else BANDW
                    act.dma_start(bias[lo:hi, :, c0:VARY],
                                  bass.AP(revd.tensor, it * (PAIR * REVW), [[0, hi - lo], [REVW, PAIR], [1, VARY - c0]])
                                  ).then_inc(s["bias_in"], 16)
                    act.dma_start(bias[lo:hi, :, VARY:c1],
                                  bass.AP(skewd.tensor, it * (PAIR * P * SKEW) + (lo * (SKEW - 1) + P - 1),
                                          [[SKEW - 1, hi - lo], [P * SKEW, PAIR], [1, c1 - VARY]])
                                  ).then_inc(s["bias_in"], 16)

            def ym_hi(t):
                act.activation(actT[:, HI, :, col(t)], ymix[:, t], ACT.Copy).then_inc(s["ymhi_done"], 1)

            def wo_hi(k):
                act.wait_ge(wor_in[k], 16)
                act.activation(wo[:, k, HI, :].rearrange("p (a c) -> p a c", a=2), woraw[:, 2 * k:2 * k + 2, 0:HALF], ACT.Copy
                               ).then_inc(s["wohi_done"], 1)

            def iteration(it, last):
                v_copy(it, 0)
                deviation(it, 1)
                qk_hi(it, 1)
                take(it, 2)
                take(it, 3)
                deviation(it, 2)
                qk_hi(it, 2)
                v_copy(it, 1)
                deviation(it, 3)
                qk_hi(it, 3)
                c_copy(it, 0)
                act.wait_ge(s["vt_done"], it + 1)
                act.activation(V[:, HI], PT[:, :].rearrange("p (t c) -> p t c", c=P), ACT.Copy).then_inc(s["vhi_done"], 1)
                exps(it, 0)
                for u in range(UNITS):
                    if u + 1 < UNITS:
                        exps(it, u + 1)
                    pt_hi(it, u)
                    if u == 6:
                        act.wait_ge(s["y_done"], it * 2 + 1)
                        squares(it, 4, zs[:, 2])
                    if u == 8:
                        deviation(it, 4)
                    if u == 9:
                        c_copy(it, 1)
                    if u == 10:
                        o_dev(it, 0)
                    if u == 12:
                        o_store(it, 0)
                    if u == 14:
                        act.wait_ge(s["y_done"], it * 2 + 2)
                        squares(it, 5, zs[:, 2])
                        if last:
                            act.wait_ge(s["proj_done"], PRIMED + NPAIR * G)
                            ym_hi(0)
                            wo_hi(0)
                if not last:
                    bias_load(it + 1)
                    o_dev(it, 1)
                    take(it + 1, 0)
                    deviation(it, 5)
                    take(it + 1, 1)
                    o_store(it, 1)
                    deviation(it + 1, 0)
                    qk_hi(it + 1, 0)
                else:
                    wo_hi(1)
                    wo_hi(2)
                    deviation(it, 5)
                    act.wait_ge(s["pv_done"], NPAIR * UNITS)
                    wo_hi(3)
                    o_dev(it, 1)
                    wo_hi(4)
                    o_store(it, 1)
                    act.wait_ge(s["zn_done"], 6 * NPAIR)
                    act.activation(osd[:, 0:1], eps[:, 0:1], ACT.Copy).then_inc(s["mix_done"], 1)
                    for k in range(5, KD):
                        wo_hi(k)
                    ym_hi(1)

            act.wait_ge(s["skew_out"], 16)
            bias_load(0)
            take(0, 0)
            take(0, 1)
            deviation(0, 0)
            qk_hi(0, 0)
            with act.Fori(0, NPAIR - 1) as it:
                iteration(it, False)
            iteration(NPAIR - 1, True)

            def hn_hi(t):
                act.wait_ge(s["tr_done"], NT + t + 1)
                act.activation(actT[:, HI, :, col(t)],
                               (SC, PT)[t % 2][:, :].rearrange("p (k c) -> p k c", c=P), ACT.Copy).then_inc(s["xhi_done"], 1)

            for t in range(NT):
                act.wait_ge(s["hadd_done"], 2 * t + 2)
                act.wait_ge(s["ym_ready"], t + 1)
                act.activation(ymix[:, t].rearrange("p k c -> p (k c)"), h[:, t, :], ACT.Square,
                               accum_out=ssx[:, t:t + 1]).then_inc(s["ssx_done"], 1)
                act.wait_ge(s["ssx_done"], NT + t + 1)
                act.activation(sdx[:, t:t + 1], ssx[:, t:t + 1], ACT.Sqrt, bias=eps[:, 0:1],
                               scale=1.0 / DM).then_inc(s["sdx_done"], 1)
                if t + 2 < NT:
                    ym_hi(t + 2)
                if t >= 1:
                    hn_hi(t - 1)
            hn_hi(NT - 1)

            with act.Fori(0, NFB) as b:
                def h_relu(g):
                    act.wait_ge(s["mm1_done"], b * (2 * FT) + (PRIMED + g + 1))
                    act.activation(relu[:, g % 2], PJ[:, g % 2], ACT.Relu).then_inc(s["relu_done"], 1)

                def h_hi(g):
                    act.wait_ge(s["hsq_done"], b * (2 * FT) + (g + 1))
                    act.activation(hid[:, HI, g // 2, half(1 - g % 2)], hsq[:, g % 2], ACT.Copy
                                   ).then_inc(s["hhi_done"], 1)

                for g in range(2 * FT):
                    h_relu(g)
                    h_hi(g)

        @block.vector
        def _(dve):
            vec = nc.vector
            vec.memset(eps[:, :], EPS).then_inc(s["masks_ok"], 1)
            vec.memset(bias[0:HD, :, BANDW - CHUNK:BANDW], NEG).then_inc(s["masks_ok"], 1)
            vec.memset(bias[HD:P, :, 0:CHUNK], NEG).then_inc(s["masks_ok"], 1)
            vec.memset(ones[:, :].bitcast(F32), 0.0).then_inc(s["mask_set"], 1)
            dve.wait_ge(s["mask_set"], 1)
            vec.memset(ones[0:HD, 0:HD].bitcast(F32), 1.0).then_inc(s["mask_set"], 1)
            vec.memset(ones[HD:P, HD:P].bitcast(F32), 1.0).then_inc(s["mask_set"], 1)
            flat = BANDW - CLIP
            dve.wait_ge(s["rel_in"], 16)
            vec.tensor_copy(rev[:, 0:flat], rb[:, NTAB - 1:NTAB].broadcast_to([NHEAD, flat])).then_inc(s["rev_built"], 1)
            vec.tensor_copy(rev[:, flat:flat + NTAB - 1], rb[:, NTAB - 2::-1]).then_inc(s["rev_built"], 1)
            vec.tensor_copy(rev[:, flat + NTAB - 1:REVW],
                            rb[:, 0:1].broadcast_to([NHEAD, REVW - flat - NTAB + 1])).then_inc(s["rev_built"], 1)

            def x_scale(t):
                dve.wait_ge(s["sdx_done"], t + 1)
                vec.reciprocal(rsx[:, t:t + 1], sdx[:, t:t + 1]).then_inc(s["rsx_done"], 1)
                dve.wait_ge(s["rsx_done"], t + 1)
                vec.scalar_tensor_tensor(xin[:, t, :], xin[:, t, :], rsx[:, t:t + 1], gB[:, :],
                                         ALU.mult, ALU.mult).then_inc(s["xs_done"], 1)

            def lo_part(t, cols):
                vec.tensor_tensor(actT[:, LO, :, cols], (SC, PT)[t % 2][:, :].rearrange("p (k c) -> p k c", c=P),
                                  actT[:, HI, :, cols].bitcast(F32), ALU.subtract).then_inc(s["xlo_done"], 1)

            dve.wait_ge(s["g_in"], 16)
            for t in range(NT):
                x_scale(t)
                if t >= 2:
                    dve.wait_ge(s["xhi_done"], t - 1)
                    lo_part(t - 2, slice((t - 2) * P, (t - 1) * P))
            for t in (NT - 2, NT - 1):
                dve.wait_ge(s["xhi_done"], t + 1)
                lo_part(t, slice(t * P, (t + 1) * P))
            dve.wait_ge(s["prm_in"], 16 * 10)
            vec.tensor_scalar(gqk[:, 0:1], gqk[:, 0:1], HD ** -0.5, None, ALU.mult).then_inc(s["prm_g"], 1)
            dve.wait_ge(s["prm_g"], 1)
            dve.wait_ge(s["masks_ok"], 3)

            def squares_lo(it, n):
                dve.wait_ge(s["sqh_done"], it * 6 + (n + 1))
                vec.tensor_tensor(sql[:, n % 2], sq[:, zbuf(n)], sqh[:, n % 2].bitcast(F32), ALU.subtract
                                  ).then_inc(s["sql_done"], 1)

            def normalise(it, n, dst, gain, view=lambda a: a):
                b = zbuf(n)
                dve.wait_ge(s["ss_read"], it * 8 + (SSORDER[n] + 2))
                vec.reciprocal(sq[:, b], sq[:, b]).then_inc(s["rs_done"], 1)
                dve.wait_ge(s["rs_done"], it * 6 + (n + 1))
                vec.scalar_tensor_tensor(dst, view(zs[:, b]), gain, view(sq[:, b]), ALU.mult, ALU.mult
                                         ).then_inc(s["zn_done"], 1)

            def qk_norm(it, n):
                normalise(it, n, zs[:, n % 2], gqk[:, n % 2:n % 2 + 1])

            def qk_lo(it, n):
                dst = (qT, kT)[n % 2]
                dve.wait_ge(s["hi_done"], it * 4 + (n + 1))
                vec.tensor_tensor(dst[:, LO, half(n // 2)], zs[:, n % 2], dst[:, HI, half(n // 2)].bitcast(F32),
                                  ALU.subtract).then_inc(s["qklo_done"], 1)

            def conv_gate(it, n):
                g = 7 + 3 * n
                dve.wait_ge(s["proj_done"], it * G + (PRIMED + g + 1))
                dve.wait_ge(s["cs_done"], it * 2 + (n + 1))
                dve.wait_ge(s["halo_done"], it * 2 + (n + 1))
                vec.tensor_tensor(ub[:, 2:HALF + 2], PJ[:, g % 2], cs[:, :], ALU.mult).then_inc(s["u_done"], 1)

            def conv_taps(it, n):
                z = zs[:, 2]
                dve.wait_ge(s["u_done"], it * 2 + (n + 1))
                dve.wait_ge(s["prm_ready"], it + 1)
                vec.tensor_scalar(z, ub[:, 2:HALF + 2], prm[:, W2_:W2_ + 1], prm[:, CB:CB + 1], ALU.mult, ALU.add
                                  ).then_inc(s["t1_done"], 1)
                dve.wait_ge(s["t1_done"], it * 2 + (n + 1))
                vec.scalar_tensor_tensor(z, ub[:, 1:HALF + 1], prm[:, W1_:W1_ + 1], z, ALU.mult, ALU.add
                                         ).then_inc(s["t2_done"], 1)
                dve.wait_ge(s["t2_done"], it * 2 + (n + 1))
                vec.scalar_tensor_tensor(z, ub[:, 0:HALF], prm[:, W0:W0 + 1], z, ALU.mult, ALU.add
                                         ).then_inc(s["t3_done"], 1)
                dve.wait_ge(s["t3_done"], it * 2 + (n + 1))
                if n == 0:
                    vec.tensor_copy(ub[:, 0:2], ub[:, HALF:HALF + 2]).then_inc(s["halo_done"], 1)

            def conv_out(it, n):
                g = 8 + 3 * n
                dve.wait_ge(s["proj_done"], it * G + (PRIMED + g + 1))
                vec.tensor_tensor(zs[:, 2], PJ[:, g % 2], zs[:, 2], ALU.mult).then_inc(s["y_done"], 1)

            def conv_norm(it, n):
                dst = ymix[:, 4 * n:4 * n + 4, bass.ds(it, 1), :].rearrange("p t o c -> p t (o c)")
                normalise(it, 4 + n, dst, prm[:, CG:CG + 1], lambda a: a.rearrange("p (t c) -> p t c", c=P))

            def scores(it, u):
                L = P * keys(u)
                wait_alone(dve, s["sc_done"], it * UNITS + (u + 1))
                vec.tensor_tensor_reduce(out=prob[:, u % 2, 0:L], in0=SC[:, 0:L], in1=bias[:, u % 2, BANDW - L:BANDW],
                                         scale=-1.0, scalar=3.0e38, op0=ALU.add, op1=ALU.min,
                                         accum_out=negm[:, u:u + 1]).then_inc(s["sm_done"], 1)

            def pt_lo(it, u):
                L = P * keys(u)
                dve.wait_ge(s["pthi_done"], it * UNITS + (u + 1))
                vec.tensor_tensor(pT[:, LO, 0:L], PT[:, 0:L], pT[:, HI, 0:L].bitcast(F32), ALU.subtract
                                  ).then_inc(s["ptlo_done"], 1)

            og = on[:, :, :].rearrange("p g (u d) -> p g u d", d=HD)

            def per_unit(a):
                return a[:, :].rearrange("p (u o) -> p u o", o=1).broadcast_to([P, 8, HD])

            def o_scale(it, g):
                dve.wait_ge(s["exp_done"], it * UNITS + 8 * (g + 1))
                vec.reciprocal(orl[:, :], esum[:, 8 * g:8 * g + 8]).then_inc(s["rl_done"], 1)
                dve.wait_ge(s["rl_done"], it * 2 + (g + 1))
                dve.wait_ge(s["pv_done"], it * UNITS + 8 * (g + 1))
                vec.tensor_tensor(og[:, g], OB[:, :].rearrange("p (u d) -> p u d", d=HD), per_unit(orl), ALU.mult
                                  ).then_inc(s["osc_done"], 1)
                dve.wait_ge(s["osc_done"], it * 2 + (g + 1))
                vec.tensor_tensor(osq[:, :], on[:, g], on[:, g], ALU.mult).then_inc(s["osq_done"], 1)
                dve.wait_ge(s["osq_done"], it * 2 + (g + 1))
                vec.tensor_reduce(oss[:, :], osq[:, :].rearrange("p (u d) -> p u d", d=HD), AX.X, ALU.add
                                  ).then_inc(s["oss_done"], 1)

            def o_norm(it, g):
                dve.wait_ge(s["osd_done"], it * 2 + (g + 1))
                vec.reciprocal(ors[:, :], osd[:, :]).then_inc(s["ors_done"], 1)
                dve.wait_ge(s["ors_done"], it * 2 + (g + 1))
                vec.tensor_tensor(og[:, g], og[:, g], per_unit(ors), ALU.mult).then_inc(s["on_done"], 1)

            def ym_lo(t):
                dve.wait_ge(s["ymhi_done"], t + 1)
                vec.tensor_tensor(actT[:, LO, :, col(t)], ymix[:, t], actT[:, HI, :, col(t)].bitcast(F32), ALU.subtract
                                  ).then_inc(s["ym_ready"], 1)

            def wo_lo(k):
                dve.wait_ge(s["wohi_done"], k + 1)
                vec.tensor_tensor(wo[:, k, LO, :].rearrange("p (a c) -> p a c", a=2), woraw[:, 2 * k:2 * k + 2, 0:HALF],
                                  wo[:, k, HI, :].rearrange("p (a c) -> p a c", a=2).bitcast(F32), ALU.subtract
                                  ).then_inc(s["wo_ready"], 1)

            def iteration(it, last):
                dve.wait_ge(s["ss_read"], it * 8 + 1)
                vec.tensor_copy(prm[:, :], prm_all[:, :, bass.ds(it, 1)].rearrange("p a o -> p (a o)")).then_inc(s["prm_ready"], 1)
                vec.memset(ub[:, 0:2], 0.0).then_inc(s["halo_done"], 1)
                qk_norm(it, 1)
                qk_lo(it, 1)
                squares_lo(it, 2)
                squares_lo(it, 3)
                qk_norm(it, 2)
                qk_lo(it, 2)
                qk_norm(it, 3)
                qk_lo(it, 3)
                dve.wait_ge(s["vhi_done"], it + 1)
                vec.tensor_tensor(V[:, LO], PT[:, :].rearrange("p (t c) -> p t c", c=P), V[:, HI].bitcast(F32),
                                  ALU.subtract).then_inc(s["vlo_done"], 1)
                dve.wait_ge(s["bias_in"], it * 64 + 64)
                scores(it, 0)
                for u in range(UNITS):
                    if u + 1 < UNITS:
                        scores(it, u + 1)
                    pt_lo(it, u)
                    if u == 3:
                        conv_gate(it, 0)
                    if u == 4:
                        conv_taps(it, 0)
                    if u == 6:
                        conv_out(it, 0)
                        squares_lo(it, 4)
                    if u == 8:
                        o_scale(it, 0)
                    if u == 9:
                        conv_norm(it, 0)
                    if u == 10:
                        o_norm(it, 0)
                    if u == 12:
                        conv_gate(it, 1)
                        conv_taps(it, 1)
                    if u == 14:
                        conv_out(it, 1)
                        squares_lo(it, 5)
                if not last:
                    o_scale(it, 1)
                    squares_lo(it + 1, 0)
                    o_norm(it, 1)
                    conv_norm(it, 1)
                    squares_lo(it + 1, 1)
                    qk_norm(it + 1, 0)
                    qk_lo(it + 1, 0)
                else:
                    ym_lo(0)
                    wo_lo(0)
                    wo_lo(1)
                    wo_lo(2)
                    o_scale(it, 1)
                    wo_lo(3)
                    o_norm(it, 1)
                    wo_lo(4)
                    conv_norm(it, 1)
                    for k in range(5, KD):
                        wo_lo(k)
                    ym_lo(1)

            squares_lo(0, 0)
            squares_lo(0, 1)
            qk_norm(0, 0)
            qk_lo(0, 0)
            with dve.Fori(0, NPAIR - 1) as it:
                iteration(it, False)
            iteration(NPAIR - 1, True)

            for t in range(NT):
                dve.wait_ge(xr_in[t], 16)
                for a in range(2):
                    if t == NT - 1 and a == 1:
                        dve.wait_ge(s["mm2_done"], 1)
                    else:
                        dve.wait_ge(s["proj_done"], PRIMED + G * NPAIR + 2 * t + a + 1)
                    vec.tensor_tensor(h[:, t, half(a)], PJ[:, a], h[:, t, half(a)], ALU.add).then_inc(s["hadd_done"], 1)
                if t + 2 < NT:
                    ym_lo(t + 2)
                if t == 0:
                    dve.wait_ge(s["g_again"], 16)
                dve.wait_ge(s["sdx_done"], NT + t + 1)
                vec.reciprocal(rsx[:, t:t + 1], sdx[:, t:t + 1]).then_inc(s["rsx_done"], 1)
                dve.wait_ge(s["rsx_done"], NT + t + 1)
                vec.scalar_tensor_tensor(ymix[:, t].rearrange("p k c -> p (k c)"), h[:, t, :], rsx[:, t:t + 1], gB[:, :],
                                         ALU.mult, ALU.mult).then_inc(s["xs_done"], 1)
                if t >= 1:
                    dve.wait_ge(s["xhi_done"], NT + t)
                    lo_part(t - 1, col(t - 1))
            dve.wait_ge(s["xhi_done"], 2 * NT)
            lo_part(NT - 1, col(NT - 1))

            with dve.Fori(0, NFB) as b:
                def h_square(g):
                    dve.wait_ge(s["relu_done"], b * (2 * FT) + (g + 1))
                    vec.scalar_tensor_tensor(hsq[:, g % 2], PJ[:, g % 2], 0.0, relu[:, g % 2], ALU.max, ALU.mult
                                             ).then_inc(s["hsq_done"], 1)

                def h_lo(g):
                    dve.wait_ge(s["hhi_done"], b * (2 * FT) + (g + 1))
                    c = half(1 - g % 2)
                    vec.tensor_tensor(hid[:, LO, g // 2, c], hsq[:, g % 2], hid[:, HI, g // 2, c].bitcast(F32),
                                      ALU.subtract).then_inc(s["hlo_done"], 1)

                for g in range(2 * FT):
                    h_square(g)
                    h_lo(g)
                for m in range(2 * NT):
                    t, a = m // 2, m % 2
                    dve.wait_ge(s["mm2_done"], b * (2 * NT) + (m + 2))
                    vec.tensor_tensor(h[:, t, half(a)], MM2BANK[2 * (t % 3) + a], h[:, t, half(a)], ALU.add
                                      ).then_inc(s["acc_done"], 1)

        @block.tensor
        def _(pe):
            mm = nc.tensor.matmul
            pe.sem_inc(s["proj_done"], PRIMED)
            pe.sem_inc(s["mm1_done"], PRIMED)
            pe.wait_ge(s["consts"], 2)

            def x_transpose(t):
                pe.wait_ge(s["xs_done"], t + 1)
                if t >= 2:
                    pe.wait_ge(s["xlo_done"], t - 1)
                bank = (SC, PT)[t % 2]
                for k in range(KD):
                    last = nc.tensor.transpose(bank[:, k * P:(k + 1) * P], xin[:, t, k * P:(k + 1) * P], ident[:, :])
                last.then_inc(s["tr_done"], 1)

            def group_product(it, g, r, first=False):
                kind, hf = GROUPS[g]
                w, k, (a, b) = ORDER.index(kind), r // 3, PASSES[r % 3]
                if r == 0:
                    if hf == 0:
                        pe.wait_ge(s["w_ready"], it * NW + (w + 1))
                    if g in (0, 1):
                        if not first:
                            pe.wait_ge(s[("u_done", "y_done")[g]], it * 2)
                    else:
                        sem, per, count = {2: ("sqh_done", 6, 1), 3: ("sqh_done", 6, 2), 4: ("vcopy_done", 2, 1),
                                           5: ("sqh_done", 6, 3), 6: ("sqh_done", 6, 4), 7: ("vcopy_done", 2, 2),
                                           8: ("cs_done", 2, 1), 9: ("u_done", 2, 1), 10: ("y_done", 2, 1),
                                           11: ("cs_done", 2, 2)}[g]
                        pe.wait_ge(s[sem], it * per + count)
                last = mm(PJ[:, g % 2], wsl[:, w % NSLOT, a, k], actT[:, b, k, half(hf)],
                          start=(r == 0), stop=(r == 3 * KD - 1))
                if r == 3 * KD - 1:
                    last.then_inc(s["proj_done"], 1)

            def project(it, g):
                for r in range(3 * KD):
                    group_product(it, g, r)

            def sum_squares(it, n):
                pe.wait_ge(s["sql_done"], it * 6 + (n + 1))
                pe.wait_ge(s["ss_read"], it * 8 + (SSORDER[n] + 1))
                mm(SS[:, :], ones[:, :], sqh[:, n % 2], start=True, stop=False)
                mm(SS[:, :], ones[:, :], sql[:, n % 2], start=False, stop=True).then_inc(s["ones_done"], 1)

            def score(it, u):
                t, hh = u // 2, u % 2
                nb = keys(u)
                hp = slice(hh * HD, (hh + 1) * HD)
                if u == 0:
                    pe.wait_ge(s["qklo_done"], it * 4 + 4)
                else:
                    pe.wait_ge(s["sm_done"], it * UNITS + u)
                for c0 in range(0, nb * P, HALF):
                    c1 = min(c0 + HALF, nb * P)
                    k0 = (t - nb + 1) * P
                    for n, (a, b) in enumerate(PASSES):
                        last = mm(SC[:, c0:c1], qT[hp, a, t * P:(t + 1) * P], kT[hp, b, k0 + c0:k0 + c1],
                                  start=(n == 0), stop=(n == 2))
                last.then_inc(s["sc_done"], 1)

            def prob_transpose(it, u):
                pe.wait_ge(s["exp_done"], it * UNITS + (u + 1))
                if u == 0:
                    pe.wait_ge(s["vlo_done"], it + 1)
                else:
                    pe.wait_ge(s["ptlo_done"], it * UNITS + u)
                for j in range(keys(u)):
                    last = nc.tensor.transpose(PT[:, j * P:(j + 1) * P], prob[:, u % 2, j * P:(j + 1) * P], ident[:, :])
                last.then_inc(s["pt_done"], 1)

            def prob_v(it, u):
                t, hh = u // 2, u % 2
                nb = keys(u)
                pe.wait_ge(s["ptlo_done"], it * UNITS + (u + 1))
                if u == 8:
                    pe.wait_ge(s["osc_done"], it * 2 + 1)
                o0 = (t % 4) * P + hh * HD
                for j in range(nb):
                    for n, (a, b) in enumerate(PASSES):
                        last = mm(OB[:, o0:o0 + HD], pT[:, a, j * P:(j + 1) * P],
                                  V[:, b, t - nb + 1 + j, hh * HD:(hh + 1) * HD],
                                  start=(j == 0 and n == 0), stop=(j == nb - 1 and n == 2))
                last.then_inc(s["pv_done"], 1)

            def o_transpose(it, g):
                pe.wait_ge(s["on_done"], it * 2 + (g + 1))
                pe.wait_ge(s["ss_read"], it * 8 + (6 + 2 * g))
                for t in range(4):
                    last = nc.tensor.transpose(SS[:, t * P:(t + 1) * P], on[:, g, t * P:(t + 1) * P], ident[:, :])
                last.then_inc(s["ot_done"], 1)

            def iteration(it, last):
                project(it, 2)
                sum_squares(it, 1)
                project(it, 3)
                project(it, 4)
                sum_squares(it, 2)
                project(it, 5)
                sum_squares(it, 3)
                project(it, 6)
                pe.wait_ge(s["vcopy_done"], it * 2 + 2)
                for t in range(NT):
                    v_t = nc.tensor.transpose(PT[:, t * P:(t + 1) * P], vT[:, t * P:(t + 1) * P], ident[:, :])
                v_t.then_inc(s["vt_done"], 1)

                n = 0

                def fill(upto):
                    for m in range(n, min(upto, 5 * 3 * KD)):
                        group_product(it, 7 + m // (3 * KD), m % (3 * KD))
                    return max(n, min(upto, 5 * 3 * KD))

                score(it, 0)
                for u in range(UNITS):
                    if u + 1 < UNITS:
                        score(it, u + 1)
                    n = fill(n + FILL[u] // 2)
                    if u >= 1:
                        prob_v(it, u - 1)
                    prob_transpose(it, u)
                    n = fill(n + FILL[u] - FILL[u] // 2)
                    if u == 7:
                        sum_squares(it, 4)
                    if u == 11:
                        o_transpose(it, 0)
                assert n == 5 * 3 * KD
                if not last:
                    group_product(it + 1, 0, 0)
                    for r in range(1, 3 * KD // 2):
                        group_product(it + 1, 0, r)
                    prob_v(it, UNITS - 1)
                    for r in range(3 * KD // 2, 3 * KD):
                        group_product(it + 1, 0, r)
                    sum_squares(it, 5)
                    project(it + 1, 1)
                    o_transpose(it, 1)
                    sum_squares(it + 1, 0)
                else:
                    sum_squares(it, 5)
                    prob_v(it, UNITS - 1)

            FILL = (8,) * 8 + (9,) * 6 + (2, 0)

            for t in range(4):
                x_transpose(t)
            pe.wait_ge(s["mask_set"], 3)
            pe.wait_ge(s["xlo_done"], 4)
            for g in (0, 1):
                for r in range(3 * KD):
                    if r in (8, 16):
                        x_transpose(4 + 2 * g + r // 16)
                    group_product(0, g, r, first=True)
            sum_squares(0, 0)
            pe.wait_ge(s["xlo_done"], NT)
            with pe.Fori(0, NPAIR - 1) as it:
                iteration(it, False)
            iteration(NPAIR - 1, True)

            def w_out_products(t, hf, k):
                for n, (a, b) in enumerate(PASSES):
                    last = mm(PJ[:, hf], actT[:, a, k, col(t)], wo[:, k, b, half(hf)],
                              start=(k == 0 and n == 0), stop=(k == KD - 1 and n == 2))
                if k == KD - 1:
                    last.then_inc(s["mm2_done" if t == NT - 1 and hf else "proj_done"], 1)

            def h_transpose(t):
                pe.wait_ge(s["xs_done"], NT + t + 1)
                if t >= 2:
                    pe.wait_ge(s["xlo_done"], NT + t - 1)
                bank = (SC, PT)[t % 2]
                for k in range(KD):
                    last = nc.tensor.transpose(bank[:, k * P:(k + 1) * P], ymix[:, t, k, :], ident[:, :])
                last.then_inc(s["tr_done"], 1)

            pe.wait_ge(s["ym_ready"], 1)
            for k in range(KD):
                pe.wait_ge(s["wo_ready"], k + 1)
                for hf in range(2):
                    w_out_products(0, hf, k)
                if k == 3:
                    o_transpose(NPAIR - 1, 1)
            for t in range(1, NT):
                pe.wait_ge(s["ym_ready"], t + 1)
                for hf in range(2):
                    pe.wait_ge(s["hadd_done"], 2 * t - 1 + hf)
                    for k in range(KD):
                        w_out_products(t, hf, k)
                h_transpose(t - 1)
            h_transpose(NT - 1)

            pe.wait_ge(s["xlo_done"], 2 * NT)
            with pe.Fori(0, NFB) as b:
                for g in range(2 * FT):
                    f = g // 2
                    if g % 2 == 0:
                        pe.wait_ge(s["w_ready"], b * ND + (N_B + D_ORDER.index(("w1", f)) + 1))
                    if g >= 2:
                        pe.wait_ge(s["hsq_done"], b * (2 * FT) + (g - 1))
                    for k in range(KD):
                        for n, (x0, x1) in enumerate(PASSES):
                            last = mm(PJ[:, g % 2], w1[:, f % 2, x0, k], actT[:, x1, k, half(1 - g % 2)],
                                      start=(k == 0 and n == 0), stop=(k == KD - 1 and n == 2))
                    last.then_inc(s["mm1_done"], 1)

                def mm2(t, a, f):
                    for n, (x0, x1) in enumerate(PASSES):
                        last = mm(MM2BANK[2 * (t % 3) + a], hid[:, x0, f, col(t)], w2[:, x1, f, half(a)],
                                  start=(f == 0 and n == 0), stop=(f == FT - 1 and n == 2))
                    if f == FT - 1:
                        last.then_inc(s["mm2_done"], 1)

                pe.wait_ge(s["w_ready"], b * ND + (N_B + ND))
                for fs in (range(FT - 1), range(FT - 1, FT)):
                    pe.wait_ge(s["hlo_done"], b * (2 * FT) + (2 * fs[-1] + 1))
                    for t in range(2):
                        for a in range(2):
                            for f in fs:
                                mm2(t, a, f)
                pe.wait_ge(s["hlo_done"], b * (2 * FT) + 2 * FT)
                for t in range(2, NT):
                    for a in range(2):
                        if t >= 3:
                            pe.wait_ge(s["acc_done"], b * (2 * NT) + (2 * (t - 3) + a + 1))
                        for f in range(FT):
                            mm2(t, a, f)


_INS = ["x", "norm_mix_g", "w_in", "conv_w", "conv_b", "q_norm_g", "k_norm_g", "rel_bias",
        "conv_out_g", "attn_out_g", "w_out", "norm_mlp_g", "w_mlp_in", "w_mlp_out"]


def kernel(**inputs):
    import numpy as np
    import concourse.bacc as bacc
    from concourse.bass_utils import run_bass_kernel_spmd

    nc = bacc.Bacc("TRN2", target_bir_lowering=False, num_devices=1)
    arrays, args = {}, []
    for name in _INS:
        a = np.ascontiguousarray(inputs[name])
        arrays[f"in_{name}"] = a
        args.append(nc.dram_tensor(f"in_{name}", a.shape, mybir.dt.from_np(a.dtype), kind="ExternalInput").ap())
    args.append(nc.dram_tensor("out_0", (1, SEQ, DM), F32, kind="ExternalOutput").ap())
    build(nc, *args)
    r = run_bass_kernel_spmd(nc, [arrays], core_ids=[0])
    return r.results[0]["out_0"]
```

```python
import concourse.bass as bass
from concourse import mybir
from contextlib import ExitStack

F32 = mybir.dt.float32
F32R = mybir.dt.float32r
ALU = mybir.AluOpType
ACT = mybir.ActivationFunctionType
AX = mybir.AxisListType

P = 128
SEQ = 1024
DM = 1024
FF = 4 * DM
CHUNK = 64
LEFT = 8
CW = DM // 2
HD = 64
NHEAD = CW // HD
NTAB = 192
CLIP = 128
EPS = 1e-6
NEG = -1e30

NT = SEQ // P
KD = DM // P
HALF = 512
NH2 = SEQ // HALF
NPAIR = CW // P
PAIR = P // HD
MAXB = LEFT * CHUNK // P + 1
BANDW = MAXB * P
UNITS = NT * PAIR
FT = 4
NFB = FF // (FT * P)
REVW = BANDW + P - 1
VARY = BANDW - 2 * P
SKEW = REVW - VARY
PASSES = ((0, 0), (0, 1), (1, 0))
HI, LO = 0, 1
CBASE = {"q": 3 * CW, "k": 4 * CW, "v": 5 * CW, "C": CW, "H": 2 * CW, "B": 0}
ORDER = ("q", "k", "v", "C", "H", "B")
NW = len(ORDER)
NSLOT = 3


def build(nc, x, norm_mix_g, w_in, conv_w, conv_b, q_norm_g, k_norm_g, rel_bias,
          conv_out_g, attn_out_g, w_out, norm_mlp_g, w_mlp_in, w_mlp_out, out):
    ctx = ExitStack()
    with ctx:
        BASE = 16512
        KB = 1024
        RA, RB, RC, RD, RE = (BASE + KB * o for o in (0, 64, 96, 128, 192))

        def plan(at):
            cur = [at]

            def put(name, shape, dt):
                size = 4
                for n in shape[1:]:
                    size *= n
                t = nc.alloc_sbuf_tensor_at(name, list(shape), dt, offset=cur[0])
                cur[0] += (size + 31) // 32 * 32
                return t
            return put, cur

        actT = nc.alloc_sbuf_tensor_at("actT", [P, 2, KD, SEQ], F32R, offset=RA)
        xin = nc.alloc_sbuf_tensor_at("xin", [P, NT, DM], F32, offset=RB)
        ymix = nc.alloc_sbuf_tensor_at("ymix", [P, NT, KD, P], F32, offset=RB)
        put, top = plan(RB)
        w1 = put("w1", [P, 2, 2, KD, P], F32R)
        relu = put("relu", [P, 2, HALF], F32)
        hsq = put("hsq", [P, 2, HALF], F32)
        assert top[0] <= RC
        h = nc.alloc_sbuf_tensor_at("h", [P, NT, DM], F32, offset=RC)
        put, top = plan(RC)
        qT = put("qT", [P, 2, SEQ], F32R)
        zs = put("zs", [P, 3, HALF], F32)
        sq = put("sq", [P, 3, HALF], F32)
        cs = put("cs", [P, HALF], F32)
        ub = put("ub", [P, HALF + 2], F32)
        on = put("on", [P, 2, HALF], F32)
        osq = put("osq", [P, HALF], F32)
        assert top[0] <= RD
        wo = nc.alloc_sbuf_tensor_at("wo", [P, KD, 2, DM], F32R, offset=RD)
        hid = nc.alloc_sbuf_tensor_at("hid", [P, 2, FT, SEQ], F32R, offset=RD)
        w2 = nc.alloc_sbuf_tensor_at("w2", [P, 2, FT, DM], F32R, offset=RD + 32 * KB)
        put, top = plan(RD)
        wsl = put("wsl", [P, NSLOT, 2, KD, P], F32R)
        WO_EARLY = NSLOT
        kT = put("kT", [P, 2, SEQ], F32R)
        V = put("V", [P, NT, PAIR, 2, HD], F32R)
        bias = put("bias", [P, PAIR, BANDW], F32)
        prob = put("prob", [P, 2, BANDW], F32)
        pT = put("pT", [P, 2, BANDW], F32R)
        sqh = put("sqh", [P, 2, HALF], F32R)
        sql = put("sql", [P, 2, HALF], F32R)
        uT = put("uT", [P, 2, P], F32)
        assert top[0] <= RE
        woraw = nc.alloc_sbuf_tensor_at("woraw", [P, 2 * KD, SEQ], F32, offset=RA)
        junk = nc.alloc_sbuf_tensor_at("junk", [P, DM], F32, offset=RD + 52 * KB)
        rb = nc.alloc_sbuf_tensor_at("rb", [NHEAD, NTAB], F32, offset=RD + 57 * KB)
        rev = nc.alloc_sbuf_tensor_at("rev", [NHEAD, REVW], F32, offset=RD + 58 * KB)
        put, top = plan(RE)
        raw = put("raw", [P, 2, KD * P], F32)
        gB = put("gB", [P, DM], F32)
        ident = put("ident", [P, P], F32)
        ones = put("ones", [P, P], F32R)
        prm_all = put("prm_all", [P, 6, NPAIR], F32)
        prm = put("prm", [P, 6], F32)
        gqk = put("gqk", [P, 2], F32)
        eps = put("eps", [P, 1], F32)
        ssx = put("ssx", [P, NT], F32)
        sdx = put("sdx", [P, NT], F32)
        rsx = put("rsx", [P, NT], F32)
        negm = put("negm", [P, UNITS], F32)
        esum = put("esum", [P, UNITS], F32)
        orl = put("orl", [P, 8], F32)
        oss = put("oss", [P, 8], F32)
        osd = put("osd", [P, 8], F32)
        ors = put("ors", [P, 8], F32)
        vT = put("vT", [P, HALF], F32)
        assert top[0] <= nc.sbuf_usable_end, (top[0], nc.sbuf_usable_end)

        def col(t):
            c = (t + NT // 2) % NT * P
            return slice(c, c + P)

        W0, W1_, W2_, CB, CG, AG = range(6)

        PJ = ctx.enter_context(nc.psum_tensor("PJ", [P, 2, HALF], F32))
        SC = ctx.enter_context(nc.psum_tensor("SC", [P, 2 * HALF], F32))
        PT = ctx.enter_context(nc.psum_tensor("PT", [P, 2 * HALF], F32))
        OB = ctx.enter_context(nc.psum_tensor("OB", [P, HALF], F32))
        SS = ctx.enter_context(nc.psum_tensor("SS", [P, HALF], F32))
        UP, UQ = OB[:, 0:2 * P].rearrange("p (b c) -> p b c", b=2), OB[:, 2 * P:4 * P]
        MM2BANK = [SC[:, 0:HALF], SC[:, HALF:2 * HALF], PT[:, 0:HALF], PT[:, HALF:2 * HALF], OB[:, :], SS[:, :]]

        revd = nc.dram_tensor("revd", [NHEAD, REVW], F32, kind="Internal").ap()
        skewd = nc.dram_tensor("skewd", [NHEAD, P, SKEW], F32, kind="Internal").ap()

        names = """
        x_in g_in prm_in rel_in rev_out skew_out bias_in x_again g_again out_written
        consts act_warm passed mask_set masks_ok prm_g rev_built
        ssx_done sdx_done rsx_done xs_done tr_done xhi_done xlo_done junk_done
        whi_done w_ready proj_done ones_done vt_done sc_done pt_done pv_done us_done uq_done oq_done ot_done
        prm_ready halo_done sql_done rs_done zn_done rsc_done znc_done qklo_done vlo_done u_done t1_done t2_done t3_done y_done
        sm_done ptlo_done rl_done osc_done osq_done oss_done ors_done on_done
        zs_done sq_done sqh_done hi_done vcopy_done cs_done vhi_done exp_done pthi_done ss_read osd_done
        wohi_done wo_ready woq_ready ymhi_done ym_ready mix_done hadd_done
        mm1_done mm2_done relu_done hsq_done hhi_done hlo_done acc_done
        """.split()
        s = {n: ctx.enter_context(nc.semaphore(n)) for n in names}
        PRIMED = 3

        def wait_alone(eng, sem, value):
            eng.wait_ge(sem, value)
            eng.sem_inc(s["passed"], 1)

        x_in = [ctx.enter_context(nc.semaphore(f"x_in{i}")) for i in range(NT)]
        raw_in = [ctx.enter_context(nc.semaphore(f"raw_in{i}")) for i in range(2)]
        wor_in = [ctx.enter_context(nc.semaphore(f"wor_in{i}")) for i in range(KD)]
        xr_in = [ctx.enter_context(nc.semaphore(f"xr_in{i}")) for i in range(NT)]

        x_t = x[0].rearrange("(t p) d -> p t d", p=P)
        out_t = out[0].rearrange("(t p) d -> p t d", p=P)
        w_in_t = w_in[0].rearrange("(k p) c -> p k c", p=P)
        w1_t = w_mlp_in[0].rearrange("(k p) f -> p k f", p=P)
        raw_k = raw[:, :, :].rearrange("p r (k c) -> p r k c", c=P)

        N_B = NPAIR * NW
        POOL_WO = (0, 1, 2, 4, 6)
        VEC_WO = (3, 5, 7)
        RAW_B = N_B // 2
        G = 2 * NW
        D_ORDER = (("w1", 0), ("w1", 1), ("w2", 0), ("w2", 1), ("w1", 2), ("w2", 2), ("w1", 3), ("w2", 3))
        ND = len(D_ORDER)

        block = ctx.enter_context(nc.Block())

        @block.sync
        def _(sp):
            def load_in(it, w, more=0):
                cols = bass.ds(it * P + (CBASE[ORDER[w]] + more * P), P)
                sp.dma_start(raw_k[:, w % 2], w_in_t[:, :, cols]).then_inc(raw_in[w % 2], 16)

            for t in range(NT):
                sp.dma_start(xin[:, t, :], x_t[:, t, :]).then_inc(x_in[t], 16)
                if t == 0:
                    sp.dma_start(gB[:, :], bass.AP(norm_mix_g.tensor, 0, [[0, P], [1, DM]])).then_inc(s["g_in"], 16)
                if t in (1, 3):
                    load_in(0, t // 2)
            for i, g in enumerate((q_norm_g, k_norm_g)):
                for r in range(PAIR):
                    sp.dma_start(gqk[r * HD:(r + 1) * HD, i:i + 1], g.rearrange("o d -> d o"),
                                 allow_slow_non_contiguous=True).then_inc(s["prm_in"], 16)
            for j, g in ((W0, conv_w[0, 0]), (W1_, conv_w[0, 1]), (W2_, conv_w[0, 2]), (CB, conv_b[0]),
                         (CG, conv_out_g[0]), (AG, attn_out_g[0])):
                sp.dma_start(prm_all[:, j, :], g.rearrange("(i p) -> p i", p=P),
                             allow_slow_non_contiguous=True).then_inc(s["prm_in"], 16)
            sp.wait_ge(s["rev_built"], 3)
            sp.dma_start(revd, rev[:, :]).then_inc(s["rev_out"], 16)
            with sp.Fori(1, NPAIR) as nxt:
                for w in range(2, NW + 2):
                    sp.wait_ge(s["w_ready"], nxt * NW + (w - 1 - NW))
                    load_in(nxt, w % NW, -1 if w < NW else 0)
            for w in range(2, NW):
                sp.wait_ge(s["w_ready"], (NPAIR - 1) * NW + w - 1)
                load_in(NPAIR - 1, w)
            sp.wait_ge(s["proj_done"], PRIMED + (NPAIR - 1) * G + 9)
            for k in range(KD):
                sp.dma_start(woraw[:, 2 * k:2 * k + 2, 0:HALF],
                             w_out[0, k * P:(k + 1) * P, :].rearrange("p (a c) -> p a c", a=2)).then_inc(wor_in[k], 16)

            def load_mlp(b, j, more=0):
                kind, f = D_ORDER[j]
                f += more * FT
                if kind == "w1":
                    sp.dma_start(raw_k[:, j % 2], w1_t[:, :, bass.ds(b * (FT * P) + f * P, P)]).then_inc(raw_in[j % 2], 16)
                else:
                    sp.dma_start(raw[:, j % 2, :], w_mlp_out[0, bass.ds(b * (FT * P) + f * P, P), :]).then_inc(raw_in[j % 2], 16)

            for j in range(2):
                sp.wait_ge(s["w_ready"], N_B - 1 + j)
                load_mlp(0, j)
            for t in range(NT):
                if t == 0:
                    sp.wait_ge(s["sc_done"], NPAIR * UNITS)
                if t == 2:
                    sp.wait_ge(s["qklo_done"], NPAIR * 4)
                if t == 3:
                    sp.wait_ge(s["mix_done"], 1)
                sp.dma_start(h[:, t, :], x_t[:, t, :]).then_inc(xr_in[t], 16)
            sp.dma_start(gB[:, :], bass.AP(norm_mlp_g.tensor, 0, [[0, P], [1, DM]])).then_inc(s["g_again"], 16)
            with sp.Fori(2, NFB + 1) as nxt:
                for j in range(2, ND + 2):
                    sp.wait_ge(s["w_ready"], nxt * ND + (N_B + j - 1 - 2 * ND))
                    load_mlp(nxt, j % ND, -2 if j < ND else -1)
            for j in range(2, ND):
                sp.wait_ge(s["w_ready"], N_B + (NFB - 1) * ND + j - 1)
                load_mlp(NFB - 1, j)
            for t in range(NT):
                sp.wait_ge(s["acc_done"], (NFB - 1) * 2 * NT + 2 * (t + 1))
                sp.dma_start(out_t[:, t, :], h[:, t, :]).then_inc(s["out_written"], 16)
            sp.wait_ge(s["out_written"], 16 * NT)

        @block.gpsimd
        def _(pool):
            nc.gpsimd.memset(ident[:, :], 0.0).then_inc(s["consts"], 1)
            pool.wait_ge(s["consts"], 1)
            nc.gpsimd.affine_select(out=ident[:, :], in_=ident[:, :], compare_op=ALU.not_equal, fill=1.0, base=0,
                                    pattern=[[-1, P]], channel_multiplier=1).then_inc(s["consts"], 1)

            with pool.Fori(0, NPAIR) as it:
                for w in range(NW):
                    sl = w % NSLOT
                    pool.wait_ge(raw_in[w % 2], it * (NW // 2 * 16) + 16 * (w // 2 + 1))
                    wait_alone(pool, s["proj_done"], it * G + (PRIMED + (w + 1 if w >= NSLOT else w - 2)))
                    nc.gpsimd.tensor_copy(wsl[:, sl, HI], raw_k[:, w % 2]).then_inc(s["whi_done"], 1)
                    pool.wait_ge(s["whi_done"], it * NW + (w + 1))
                    nc.gpsimd.tensor_tensor(wsl[:, sl, LO], raw_k[:, w % 2], wsl[:, sl, HI].bitcast(F32),
                                            ALU.subtract).then_inc(s["w_ready"], 1)
            for k in POOL_WO:
                pool.wait_ge(s["wohi_done"], k + 1)
                nc.gpsimd.tensor_tensor(wo[:, k, LO, :].rearrange("p (a c) -> p a c", a=2), woraw[:, 2 * k:2 * k + 2, 0:HALF],
                                        wo[:, k, HI, :].rearrange("p (a c) -> p a c", a=2).bitcast(F32), ALU.subtract
                                        ).then_inc(s["woq_ready"], 1)
            pool.wait_ge(s["tr_done"], NT + NT // 2)
            with pool.Fori(0, NFB) as b:
                for j, (kind, f) in enumerate(D_ORDER):
                    pool.wait_ge(raw_in[j % 2], b * (ND // 2 * 16) + 16 * (RAW_B + j // 2 + 1))
                    if kind == "w1":
                        wait_alone(pool, s["mm1_done"], b * (2 * FT) + (PRIMED + 2 * f - 2))
                        hi, lo, src = w1[:, f % 2, HI], w1[:, f % 2, LO], raw_k[:, j % 2]
                    else:
                        wait_alone(pool, s["mm2_done"], b * (2 * NT) + 1)
                        hi, lo, src = w2[:, HI, f], w2[:, LO, f], raw[:, j % 2, :]
                    nc.gpsimd.tensor_copy(hi, src).then_inc(s["whi_done"], 1)
                    pool.wait_ge(s["whi_done"], b * ND + (N_B + j + 1))
                    nc.gpsimd.tensor_tensor(lo, src, hi.bitcast(F32), ALU.subtract).then_inc(s["w_ready"], 1)

        GROUPS = (("q", 0), ("k", 0), ("v", 0), ("q", 1), ("k", 1), ("v", 1),
                  ("C", 0), ("H", 0), ("B", 0), ("C", 1), ("H", 1), ("B", 1))
        QKGROUP = (0, 1, 3, 4)
        TURN = (-1, 0, 2, 3, 4, 6)
        OTURN = (5, 9)
        LAST_OTURN = 7
        NLEAD = 4
        REST = (G - NLEAD) * 3 * KD
        FILL = (14,) * 8 + (15,) * 8
        FILL_LAST = (14,) * 12 + (12, 12, 0, 0)

        def half(n):
            return slice(n * HALF, (n + 1) * HALF)

        def zbuf(n):
            return n % 2 if n < 4 else 2

        def keys(u):
            return min(u // 2 + 1, MAXB)

        def score_at(u):
            return P if keys(u) == MAXB else 0

        @block.scalar
        def _(act):
            act.sem_inc(s["ss_read"], 2)
            act.dma_start(rb[:, :], rel_bias[0]).then_inc(s["rel_in"], 16)
            act.wait_ge(s["masks_ok"], 3)
            act.activation(osd[:, 0:1], eps[:, 0:1], ACT.Sqrt).then_inc(s["act_warm"], 1)

            def x_stats(t):
                act.wait_ge(x_in[t], 16)
                if t:
                    act.wait_ge(s["ssx_done"], t)
                act.activation(junk[:, :], xin[:, t, :], ACT.Square, accum_out=ssx[:, t:t + 1]).then_inc(s["ssx_done"], 1)
                act.wait_ge(s["ssx_done"], t + 1)
                act.activation(sdx[:, t:t + 1], ssx[:, t:t + 1], ACT.Sqrt, bias=eps[:, 0:1],
                               scale=1.0 / DM).then_inc(s["sdx_done"], 1)

            def x_hi(t):
                act.wait_ge(s["tr_done"], t + 1)
                act.activation(actT[:, HI, :, t * P:(t + 1) * P],
                               (SC, PT)[t % 2][:, :].rearrange("p (k c) -> p k c", c=P), ACT.Copy).then_inc(s["xhi_done"], 1)

            for t in range(NT):
                x_stats(t)
                if t >= 2:
                    x_hi(t - 2)

            def squares(it, n, src):
                act.activation(sq[:, zbuf(n)], src, ACT.Square).then_inc(s["sq_done"], 1)
                act.activation(sqh[:, n % 2], src, ACT.Square).then_inc(s["sqh_done"], 1)

            def take(it, n):
                if n >= 2:
                    act.wait_ge(s["qklo_done"], it * 4 + (n - 1))
                g = QKGROUP[n]
                act.wait_ge(s["proj_done"], it * G + (PRIMED + g + 1))
                act.activation(zs[:, n % 2], PJ[:, g % 2], ACT.Copy).then_inc(s["zs_done"], 1)
                squares(it, n, PJ[:, g % 2])

            def deviation(it, n):
                act.wait_ge(s["ones_done"], it * 6 + (n + 1))
                act.activation(sq[:, zbuf(n)], SS[:, :], ACT.Sqrt, bias=eps[:, 0:1], scale=1.0 / HD).then_inc(s["ss_read"], 1)

            def qk_hi(it, n):
                act.wait_ge(s["zn_done"], it * 4 + (n + 1))
                act.activation((qT, kT)[n % 2][:, HI, half(n // 2)], zs[:, n % 2], ACT.Copy).then_inc(s["hi_done"], 1)

            def v_copy(it, n):
                g = 2 + 3 * n
                act.wait_ge(s["proj_done"], it * G + (PRIMED + g + 1))
                act.activation(vT[:, :], PJ[:, g % 2], ACT.Copy).then_inc(s["vcopy_done"], 1)

            def v_hi(it, n):
                act.wait_ge(s["vt_done"], it * 2 + (n + 1))
                act.activation(V[:, 4 * n:4 * n + 4, :, HI],
                               PT[:, HALF:SEQ].rearrange("p (t a d) -> p t a d", t=4, a=PAIR), ACT.Copy
                               ).then_inc(s["vhi_done"], 1)

            def c_copy(it, n):
                g = 6 + 3 * n
                act.wait_ge(s["proj_done"], it * G + (PRIMED + g + 1))
                if n:
                    act.wait_ge(s["u_done"], it * 2 + 1)
                act.activation(cs[:, :], PJ[:, g % 2], ACT.Copy).then_inc(s["cs_done"], 1)

            def exps(it, u):
                L = P * keys(u)
                act.wait_ge(s["sm_done"], it * UNITS + (u + 1))
                act.activation(prob[:, u % 2, 0:L], prob[:, u % 2, 0:L], ACT.Exp, bias=negm[:, u:u + 1], scale=-1.0,
                               accum_out=esum[:, u:u + 1]).then_inc(s["exp_done"], 1)

            def pt_hi(it, u):
                L = P * keys(u)
                act.wait_ge(s["pt_done"], it * UNITS + (u + 1))
                act.activation(pT[:, HI, 0:L], PT[:, 0:L], ACT.Copy).then_inc(s["pthi_done"], 1)

            def o_dev(it, g):
                act.wait_ge(s["oss_done"], it * 2 + (g + 1))
                act.activation(osd[:, :], oss[:, :], ACT.Sqrt, bias=eps[:, 0:1], scale=1.0 / HD).then_inc(s["osd_done"], 1)

            def o_store(it, g):
                act.wait_ge(s["ot_done"], it * 2 + (g + 1))
                act.activation(ymix[:, 4 * g:4 * g + 4, bass.ds(it + NPAIR, 1), :].rearrange("p t o c -> p t (o c)"),
                               SS[:, :].rearrange("p (t c) -> p t c", c=P), ACT.Copy,
                               scale=prm[:, AG:AG + 1]).then_inc(s["ss_read"], 1)

            def bias_load(it):
                for lo, hi, c0 in ((0, HD, 0), (HD, P, CHUNK)):
                    c1 = BANDW - CHUNK if lo == 0 else BANDW
                    act.dma_start(bias[lo:hi, :, c0:VARY],
                                  bass.AP(revd.tensor, it * (PAIR * REVW), [[0, hi - lo], [REVW, PAIR], [1, VARY - c0]])
                                  ).then_inc(s["bias_in"], 16)
                    act.dma_start(bias[lo:hi, :, VARY:c1],
                                  bass.AP(skewd.tensor, it * (PAIR * P * SKEW) + (lo * (SKEW - 1) + P - 1),
                                          [[SKEW - 1, hi - lo], [P * SKEW, PAIR], [1, c1 - VARY]])
                                  ).then_inc(s["bias_in"], 16)

            def ym_hi(t):
                act.activation(actT[:, HI, :, col(t)], ymix[:, t], ACT.Copy).then_inc(s["ymhi_done"], 1)

            def wo_hi(k):
                act.wait_ge(wor_in[k], 16)
                act.activation(wo[:, k, HI, :].rearrange("p (a c) -> p a c", a=2), woraw[:, 2 * k:2 * k + 2, 0:HALF], ACT.Copy
                               ).then_inc(s["wohi_done"], 1)

            def iteration(it, last):
                exps(it, 0)
                for u in range(UNITS):
                    if u + 1 < UNITS:
                        exps(it, u + 1)
                    pt_hi(it, u)
                    if u == 0:
                        take(it, 2)
                    if u == 1:
                        deviation(it, 2)
                    if u == 2:
                        take(it, 3)
                    if u == 3:
                        qk_hi(it, 2)
                        v_copy(it, 1)
                    if u == 4:
                        deviation(it, 3)
                        v_hi(it, 1)
                    if u == 5:
                        c_copy(it, 0)
                    if u == 6:
                        qk_hi(it, 3)
                    if u == 9:
                        act.wait_ge(s["y_done"], it * 2 + 1)
                        squares(it, 4, zs[:, 2])
                    if u == 10:
                        o_dev(it, 0)
                        c_copy(it, 1)
                    if u == 11:
                        deviation(it, 4)
                    if u == 12:
                        o_store(it, 0)
                    if u == 13 and last:
                        act.wait_ge(s["proj_done"], PRIMED + NPAIR * G)
                        act.wait_ge(s["ss_read"], it * 8 + (OTURN[0] + 3))
                        act.wait_ge(s["znc_done"], it * 2 + 1)
                        ym_hi(0)
                        wo_hi(0)
                    if u == 13:
                        act.wait_ge(s["y_done"], it * 2 + 2)
                        squares(it, 5, zs[:, 2])
                    if u == 14 and not last:
                        take(it + 1, 0)
                        deviation(it, 5)
                    if u == 14 and last:
                        ym_hi(1)
                        wo_hi(1)
                if not last:
                    deviation(it + 1, 0)
                    take(it + 1, 1)
                    bias_load(it + 1)
                    qk_hi(it + 1, 0)
                    deviation(it + 1, 1)
                    v_copy(it + 1, 0)
                    o_dev(it, 1)
                    qk_hi(it + 1, 1)
                    v_hi(it + 1, 0)
                    o_store(it, 1)
                else:
                    wo_hi(2)
                    deviation(it, 5)
                    act.wait_ge(s["pv_done"], NPAIR * UNITS)
                    wo_hi(3)
                    wo_hi(4)
                    o_dev(it, 1)
                    for k in range(5, KD):
                        wo_hi(k)
                    o_store(it, 1)
                    act.wait_ge(s["znc_done"], 2 * NPAIR)
                    act.activation(osd[:, 0:1], eps[:, 0:1], ACT.Copy).then_inc(s["mix_done"], 1)
                    ym_hi(2)
                    ym_hi(3)

            act.wait_ge(s["rev_out"], 16)
            act.dma_start(skewd, bass.AP(revd.tensor, VARY, [[REVW, NHEAD], [0, P], [1, SKEW]])).then_inc(s["skew_out"], 16)
            take(0, 0)
            x_hi(NT - 2)
            x_hi(NT - 1)
            take(0, 1)
            deviation(0, 0)
            qk_hi(0, 0)
            deviation(0, 1)
            v_copy(0, 0)
            act.wait_ge(s["skew_out"], 16)
            bias_load(0)
            v_hi(0, 0)
            qk_hi(0, 1)
            with act.Fori(0, NPAIR - 1) as it:
                iteration(it, False)
            iteration(NPAIR - 1, True)

            def hn_hi(t):
                act.wait_ge(s["tr_done"], NT + t + 1)
                act.activation(actT[:, HI, :, col(t)],
                               (PT, SC)[t % 2][:, :].rearrange("p (k c) -> p k c", c=P), ACT.Copy).then_inc(s["xhi_done"], 1)

            for t in range(NT):
                act.wait_ge(s["hadd_done"], 2 * t + 2)
                act.wait_ge(s["ym_ready"], t + 1)
                act.activation(ymix[:, t].rearrange("p k c -> p (k c)"), h[:, t, :], ACT.Square,
                               accum_out=ssx[:, t:t + 1]).then_inc(s["ssx_done"], 1)
                act.wait_ge(s["ssx_done"], NT + t + 1)
                act.activation(sdx[:, t:t + 1], ssx[:, t:t + 1], ACT.Sqrt, bias=eps[:, 0:1],
                               scale=1.0 / DM).then_inc(s["sdx_done"], 1)
                if t + 4 < NT:
                    ym_hi(t + 4)
                if t >= 1:
                    hn_hi(t - 1)
            hn_hi(NT - 1)

            with act.Fori(0, NFB) as b:
                def h_relu(g):
                    act.wait_ge(s["mm1_done"], b * (2 * FT) + (PRIMED + g + 1))
                    act.activation(relu[:, g % 2], PJ[:, g % 2], ACT.Relu).then_inc(s["relu_done"], 1)

                def h_hi(g):
                    act.wait_ge(s["hsq_done"], b * (2 * FT) + (g + 1))
                    act.activation(hid[:, HI, g // 2, half(1 - g % 2)], hsq[:, g % 2], ACT.Copy
                                   ).then_inc(s["hhi_done"], 1)

                for g in range(2 * FT):
                    h_relu(g)
                    h_hi(g)

        @block.vector
        def _(dve):
            vec = nc.vector
            vec.memset(eps[:, :], EPS).then_inc(s["masks_ok"], 1)
            vec.memset(bias[0:HD, :, BANDW - CHUNK:BANDW], NEG).then_inc(s["masks_ok"], 1)
            vec.memset(bias[HD:P, :, 0:CHUNK], NEG).then_inc(s["masks_ok"], 1)
            vec.memset(ones[:, :].bitcast(F32), 0.0).then_inc(s["mask_set"], 1)
            dve.wait_ge(s["mask_set"], 1)
            vec.memset(ones[0:HD, 0:HD].bitcast(F32), 1.0).then_inc(s["mask_set"], 1)
            vec.memset(ones[HD:P, HD:P].bitcast(F32), 1.0).then_inc(s["mask_set"], 1)
            flat = BANDW - CLIP
            dve.wait_ge(s["rel_in"], 16)
            vec.tensor_copy(rev[:, 0:flat], rb[:, NTAB - 1:NTAB].broadcast_to([NHEAD, flat])).then_inc(s["rev_built"], 1)
            vec.tensor_copy(rev[:, flat:flat + NTAB - 1], rb[:, NTAB - 2::-1]).then_inc(s["rev_built"], 1)
            vec.tensor_copy(rev[:, flat + NTAB - 1:REVW],
                            rb[:, 0:1].broadcast_to([NHEAD, REVW - flat - NTAB + 1])).then_inc(s["rev_built"], 1)

            def x_scale(t):
                dve.wait_ge(s["sdx_done"], t + 1)
                vec.reciprocal(rsx[:, t:t + 1], sdx[:, t:t + 1]).then_inc(s["rsx_done"], 1)
                dve.wait_ge(s["rsx_done"], t + 1)
                vec.scalar_tensor_tensor(xin[:, t, :], xin[:, t, :], rsx[:, t:t + 1], gB[:, :],
                                         ALU.mult, ALU.mult).then_inc(s["xs_done"], 1)

            def lo_part(t, cols, banks=(SC, PT)):
                vec.tensor_tensor(actT[:, LO, :, cols], banks[t % 2][:, :].rearrange("p (k c) -> p k c", c=P),
                                  actT[:, HI, :, cols].bitcast(F32), ALU.subtract).then_inc(s["xlo_done"], 1)

            dve.wait_ge(s["g_in"], 16)
            for t in range(NT):
                x_scale(t)
                if t >= 2:
                    dve.wait_ge(s["xhi_done"], t - 1)
                    lo_part(t - 2, slice((t - 2) * P, (t - 1) * P))
            def squares_lo(it, n):
                dve.wait_ge(s["sqh_done"], it * 6 + (n + 1))
                vec.tensor_tensor(sql[:, n % 2], sq[:, zbuf(n)], sqh[:, n % 2].bitcast(F32), ALU.subtract
                                  ).then_inc(s["sql_done"], 1)

            def inverse(it, n, part=None, extra=0):
                b = zbuf(n)
                c = slice(0, HALF) if part is None else slice(part * (HALF // 2), (part + 1) * (HALF // 2))
                if part != 1:
                    dve.wait_ge(s["ss_read"], it * 8 + (TURN[n] + 3 + extra))
                op = vec.reciprocal(sq[:, b, c], sq[:, b, c])
                if part != 0:
                    op.then_inc(s["rs_done" if n < 4 else "rsc_done"], 1)

            def qk_scale(it, n):
                dve.wait_ge(s["rs_done"], it * 4 + (n + 1))
                vec.scalar_tensor_tensor(zs[:, n % 2], zs[:, n % 2], gqk[:, n % 2:n % 2 + 1], sq[:, n % 2],
                                         ALU.mult, ALU.mult).then_inc(s["zn_done"], 1)

            def qk_lo(it, n):
                dst = (qT, kT)[n % 2]
                dve.wait_ge(s["hi_done"], it * 4 + (n + 1))
                vec.tensor_tensor(dst[:, LO, half(n // 2)], zs[:, n % 2], dst[:, HI, half(n // 2)].bitcast(F32),
                                  ALU.subtract).then_inc(s["qklo_done"], 1)

            def conv_gate(it, n):
                g = 7 + 3 * n
                dve.wait_ge(s["proj_done"], it * G + (PRIMED + g + 1))
                dve.wait_ge(s["cs_done"], it * 2 + (n + 1))
                dve.wait_ge(s["halo_done"], it * 2 + (n + 1))
                vec.tensor_tensor(ub[:, 2:HALF + 2], PJ[:, g % 2], cs[:, :], ALU.mult).then_inc(s["u_done"], 1)

            def conv_tap(it, n, i):
                z = zs[:, 2]
                if i == 0:
                    if n:
                        dve.wait_ge(s["znc_done"], it * 2 + 1)
                    dve.wait_ge(s["u_done"], it * 2 + (n + 1))
                    dve.wait_ge(s["prm_ready"], it + 1)
                    vec.tensor_scalar(z, ub[:, 2:HALF + 2], prm[:, W2_:W2_ + 1], prm[:, CB:CB + 1], ALU.mult, ALU.add
                                      ).then_inc(s["t1_done"], 1)
                if i == 1:
                    dve.wait_ge(s["t1_done"], it * 2 + (n + 1))
                    vec.scalar_tensor_tensor(z, ub[:, 1:HALF + 1], prm[:, W1_:W1_ + 1], z, ALU.mult, ALU.add
                                             ).then_inc(s["t2_done"], 1)
                if i == 2:
                    dve.wait_ge(s["t2_done"], it * 2 + (n + 1))
                    vec.scalar_tensor_tensor(z, ub[:, 0:HALF], prm[:, W0:W0 + 1], z, ALU.mult, ALU.add
                                             ).then_inc(s["t3_done"], 1)
                    dve.wait_ge(s["t3_done"], it * 2 + (n + 1))
                    if n == 0:
                        vec.tensor_copy(ub[:, 0:2], ub[:, HALF:HALF + 2]).then_inc(s["halo_done"], 1)

            def conv_out(it, n):
                g = 8 + 3 * n
                dve.wait_ge(s["proj_done"], it * G + (PRIMED + g + 1))
                vec.tensor_tensor(zs[:, 2], PJ[:, g % 2], zs[:, 2], ALU.mult).then_inc(s["y_done"], 1)

            def conv_scale(it, n):
                dve.wait_ge(s["rsc_done"], it * 2 + (n + 1))
                vec.scalar_tensor_tensor(ymix[:, 4 * n:4 * n + 4, bass.ds(it, 1), :].rearrange("p t o c -> p t (o c)"),
                                         zs[:, 2].rearrange("p (t c) -> p t c", c=P), prm[:, CG:CG + 1],
                                         sq[:, 2].rearrange("p (t c) -> p t c", c=P), ALU.mult, ALU.mult
                                         ).then_inc(s["znc_done"], 1)

            def v_lo(it, n):
                dve.wait_ge(s["vhi_done"], it * 2 + (n + 1))
                t = slice(4 * n, 4 * n + 4)
                vec.tensor_tensor(V[:, t, :, LO], PT[:, HALF:SEQ].rearrange("p (t a d) -> p t a d", t=4, a=PAIR),
                                  V[:, t, :, HI].bitcast(F32), ALU.subtract).then_inc(s["vlo_done"], 1)

            def scores(it, u):
                L = P * keys(u)
                wait_alone(dve, s["sc_done"], it * UNITS + (u + 1))
                c0 = score_at(u)
                vec.tensor_tensor_reduce(out=prob[:, u % 2, 0:L], in0=SC[:, c0:c0 + L], in1=bias[:, u % 2, BANDW - L:BANDW],
                                         scale=-1.0, scalar=3.0e38, op0=ALU.add, op1=ALU.min,
                                         accum_out=negm[:, u:u + 1]).then_inc(s["sm_done"], 1)

            def pt_lo(it, u):
                L = P * keys(u)
                dve.wait_ge(s["pthi_done"], it * UNITS + (u + 1))
                vec.tensor_tensor(pT[:, LO, 0:L], PT[:, 0:L], pT[:, HI, 0:L].bitcast(F32), ALU.subtract
                                  ).then_inc(s["ptlo_done"], 1)

            def u_sum(it, u):
                dve.wait_ge(s["pv_done"], it * UNITS + (u + 1))
                if u >= 2:
                    dve.wait_ge(s["uq_done"], it * UNITS + (u - 1))
                vec.tensor_reduce(uT[:, u % 2], UP.rearrange("p b c -> p c b"), AX.X, ALU.add
                                  ).then_inc(s["us_done"], 1)

            og = on[:, :, :].rearrange("p g (u d) -> p g u d", d=HD)

            def o_sum(it, j):
                dve.wait_ge(s["uq_done"], it * UNITS + 2 * (j + 1))
                vec.tensor_reduce(og[:, j // 4, 2 * (j % 4):2 * (j % 4) + 2], UQ.rearrange("p (u a d) -> p u d a", u=2, a=2),
                                  AX.X, ALU.add).then_inc(s["oq_done"], 1)

            def per_unit(a):
                return a[:, :].rearrange("p (u o) -> p u o", o=1).broadcast_to([P, 8, HD])

            def o_scale(it, g):
                dve.wait_ge(s["exp_done"], it * UNITS + 8 * (g + 1))
                vec.reciprocal(orl[:, :], esum[:, 8 * g:8 * g + 8]).then_inc(s["rl_done"], 1)
                dve.wait_ge(s["rl_done"], it * 2 + (g + 1))
                dve.wait_ge(s["oq_done"], it * (UNITS // 2) + 4 * (g + 1))
                vec.tensor_tensor(og[:, g], og[:, g], per_unit(orl), ALU.mult).then_inc(s["osc_done"], 1)
                dve.wait_ge(s["osc_done"], it * 2 + (g + 1))
                vec.tensor_tensor(osq[:, :], on[:, g], on[:, g], ALU.mult).then_inc(s["osq_done"], 1)
                dve.wait_ge(s["osq_done"], it * 2 + (g + 1))
                vec.tensor_reduce(oss[:, :], osq[:, :].rearrange("p (u d) -> p u d", d=HD), AX.X, ALU.add
                                  ).then_inc(s["oss_done"], 1)

            def o_norm(it, g):
                dve.wait_ge(s["osd_done"], it * 2 + (g + 1))
                vec.reciprocal(ors[:, :], osd[:, :]).then_inc(s["ors_done"], 1)
                dve.wait_ge(s["ors_done"], it * 2 + (g + 1))
                vec.tensor_tensor(og[:, g], og[:, g], per_unit(ors), ALU.mult).then_inc(s["on_done"], 1)

            def ym_lo(t):
                dve.wait_ge(s["ymhi_done"], t + 1)
                vec.tensor_tensor(actT[:, LO, :, col(t)], ymix[:, t], actT[:, HI, :, col(t)].bitcast(F32), ALU.subtract
                                  ).then_inc(s["ym_ready"], 1)

            def wo_lo(k):
                dve.wait_ge(s["wohi_done"], k + 1)
                vec.tensor_tensor(wo[:, k, LO, :].rearrange("p (a c) -> p a c", a=2), woraw[:, 2 * k:2 * k + 2, 0:HALF],
                                  wo[:, k, HI, :].rearrange("p (a c) -> p a c", a=2).bitcast(F32), ALU.subtract
                                  ).then_inc(s["wo_ready"], 1)

            def extras(it, at, last):
                if at == "0b":
                    squares_lo(it, 2)
                if at == "1b":
                    inverse(it, 2, 0)
                if at == "2a":
                    inverse(it, 2, 1)
                if at == "2b":
                    squares_lo(it, 3)
                if at == "3a":
                    qk_scale(it, 2)
                if at == "3b":
                    qk_lo(it, 2)
                if at == "4b":
                    inverse(it, 3, 0)
                if at == "5a":
                    inverse(it, 3, 1)
                if at == "5b":
                    qk_scale(it, 3)
                if at == "6a":
                    v_lo(it, 1)
                if at == "6b":
                    qk_lo(it, 3)
                if at == "7a":
                    conv_gate(it, 0)
                if at == "7b":
                    conv_tap(it, 0, 0)
                    conv_tap(it, 0, 1)
                if at == "8a":
                    conv_tap(it, 0, 2)
                if at == "9a":
                    conv_out(it, 0)
                if at == "9b":
                    o_scale(it, 0)
                if at == "10a":
                    squares_lo(it, 4)
                if at == "10b":
                    o_norm(it, 0)
                if at == "11b":
                    inverse(it, 4, 0)
                if at == "12a":
                    inverse(it, 4, 1)
                if at == "12b":
                    conv_scale(it, 0)
                if at == "11b":
                    conv_gate(it, 1)
                if at == "12b":
                    conv_tap(it, 1, 0)
                if at == "13a":
                    conv_tap(it, 1, 1)
                    conv_tap(it, 1, 2)
                if at == "13b":
                    conv_out(it, 1)
                if at == "14a" and not last:
                    squares_lo(it, 5)
                if at == "14a" and last:
                    ym_lo(0)
                if at == "15a" and last:
                    ym_lo(1)
                    squares_lo(it, 5)
                if at == "15a" and not last:
                    squares_lo(it + 1, 0)
                    inverse(it, 5, 0)
                if at == "15b" and not last:
                    inverse(it, 5, 1)

            def iteration(it, last):
                dve.wait_ge(s["ss_read"], it * 8 + 4)
                vec.tensor_copy(prm[:, :], prm_all[:, :, bass.ds(it, 1)].rearrange("p a o -> p (a o)")).then_inc(s["prm_ready"], 1)
                vec.memset(ub[:, 0:2], 0.0).then_inc(s["halo_done"], 1)
                dve.wait_ge(s["bias_in"], it * 64 + 64)
                scores(it, 0)
                for u in range(UNITS):
                    if u % 2 and u >= 3:
                        o_sum(it, (u - 3) // 2)
                    if u + 1 < UNITS:
                        scores(it, u + 1)
                    if u >= 1:
                        u_sum(it, u - 1)
                    extras(it, f"{u}a", last)
                    pt_lo(it, u)
                    extras(it, f"{u}b", last)
                if not last:
                    u_sum(it, UNITS - 1)
                    conv_scale(it, 1)
                    inverse(it + 1, 0, 0)
                    squares_lo(it + 1, 1)
                    inverse(it + 1, 0, 1)
                    qk_scale(it + 1, 0)
                    o_sum(it, UNITS // 2 - 1)
                    o_scale(it, 1)
                    inverse(it + 1, 1)
                    qk_scale(it + 1, 1)
                    qk_lo(it + 1, 0)
                    o_norm(it, 1)
                    qk_lo(it + 1, 1)
                    v_lo(it + 1, 0)
                else:
                    u_sum(it, UNITS - 1)
                    o_sum(it, UNITS // 2 - 1)
                    o_scale(it, 1)
                    wo_lo(3)
                    o_norm(it, 1)
                    wo_lo(5)
                    inverse(it, 5)
                    conv_scale(it, 1)
                    wo_lo(7)
                    ym_lo(2)
                    ym_lo(3)

            dve.wait_ge(s["masks_ok"], 3)
            squares_lo(0, 0)
            for t in (NT - 2, NT - 1):
                dve.wait_ge(s["xhi_done"], t + 1)
                lo_part(t, slice(t * P, (t + 1) * P))
            dve.wait_ge(s["prm_in"], 16 * 10)
            vec.tensor_scalar(gqk[:, 0:1], gqk[:, 0:1], HD ** -0.5, None, ALU.mult).then_inc(s["prm_g"], 1)
            dve.wait_ge(s["prm_g"], 1)
            squares_lo(0, 1)
            inverse(0, 0, extra=1)
            qk_scale(0, 0)
            inverse(0, 1, extra=1)
            qk_scale(0, 1)
            qk_lo(0, 0)
            v_lo(0, 0)
            qk_lo(0, 1)
            with dve.Fori(0, NPAIR - 1) as it:
                iteration(it, False)
            iteration(NPAIR - 1, True)

            for t in range(NT):
                dve.wait_ge(xr_in[t], 16)
                for a in range(2):
                    if t == NT - 1 and a == 1:
                        dve.wait_ge(s["mm2_done"], 1)
                    else:
                        dve.wait_ge(s["proj_done"], PRIMED + G * NPAIR + 2 * t + a + 1)
                    vec.tensor_tensor(h[:, t, half(a)], SC[:, half(a)] if t == 1 else PJ[:, a], h[:, t, half(a)], ALU.add).then_inc(s["hadd_done"], 1)
                if t + 4 < NT:
                    ym_lo(t + 4)
                if t == 0:
                    dve.wait_ge(s["g_again"], 16)
                dve.wait_ge(s["sdx_done"], NT + t + 1)
                vec.reciprocal(rsx[:, t:t + 1], sdx[:, t:t + 1]).then_inc(s["rsx_done"], 1)
                dve.wait_ge(s["rsx_done"], NT + t + 1)
                vec.scalar_tensor_tensor(ymix[:, t].rearrange("p k c -> p (k c)"), h[:, t, :], rsx[:, t:t + 1], gB[:, :],
                                         ALU.mult, ALU.mult).then_inc(s["xs_done"], 1)
                if t >= 1:
                    dve.wait_ge(s["xhi_done"], NT + t)
                    lo_part(t - 1, col(t - 1), (PT, SC))
            dve.wait_ge(s["xhi_done"], 2 * NT)
            lo_part(NT - 1, col(NT - 1), (PT, SC))

            with dve.Fori(0, NFB) as b:
                def h_square(g):
                    dve.wait_ge(s["relu_done"], b * (2 * FT) + (g + 1))
                    vec.scalar_tensor_tensor(hsq[:, g % 2], PJ[:, g % 2], 0.0, relu[:, g % 2], ALU.max, ALU.mult
                                             ).then_inc(s["hsq_done"], 1)

                def h_lo(g):
                    dve.wait_ge(s["hhi_done"], b * (2 * FT) + (g + 1))
                    c = half(1 - g % 2)
                    vec.tensor_tensor(hid[:, LO, g // 2, c], hsq[:, g % 2], hid[:, HI, g // 2, c].bitcast(F32),
                                      ALU.subtract).then_inc(s["hlo_done"], 1)

                for g in range(2 * FT):
                    h_square(g)
                    h_lo(g)
                for m in range(2 * NT):
                    t, a = m // 2, m % 2
                    dve.wait_ge(s["mm2_done"], b * (2 * NT) + (m + 2))
                    vec.tensor_tensor(h[:, t, half(a)], MM2BANK[2 * (t % 3) + a], h[:, t, half(a)], ALU.add
                                      ).then_inc(s["acc_done"], 1)

        @block.tensor
        def _(pe):
            mm = nc.tensor.matmul
            pe.sem_inc(s["proj_done"], PRIMED)
            pe.sem_inc(s["mm1_done"], PRIMED)
            pe.wait_ge(s["consts"], 2)

            def x_transpose(t):
                pe.wait_ge(s["xs_done"], t + 1)
                if t >= 2:
                    pe.wait_ge(s["xlo_done"], t - 1)
                bank = (SC, PT)[t % 2]
                for k in range(KD):
                    last = nc.tensor.transpose(bank[:, k * P:(k + 1) * P], xin[:, t, k * P:(k + 1) * P], ident[:, :])
                last.then_inc(s["tr_done"], 1)

            def group_product(it, g, r, first=False, cols=slice(0, HALF)):
                kind, hf = GROUPS[g]
                w, k, (a, b) = ORDER.index(kind), r // 3, PASSES[r % 3]
                if r == 0:
                    if hf == 0:
                        pe.wait_ge(s["w_ready"], it * NW + (w + 1))
                    if g in (0, 1):
                        if not first:
                            pe.wait_ge(s[("u_done", "y_done")[g]], it * 2)
                    else:
                        sem, per, count = {2: ("sqh_done", 6, 1), 3: ("sqh_done", 6, 2), 4: ("vcopy_done", 2, 1),
                                           5: ("sqh_done", 6, 3), 6: ("sqh_done", 6, 4), 7: ("vcopy_done", 2, 2),
                                           8: ("cs_done", 2, 1), 9: ("u_done", 2, 1), 10: ("y_done", 2, 1),
                                           11: ("cs_done", 2, 2)}[g]
                        pe.wait_ge(s[sem], it * per + count)
                c = slice(hf * HALF + cols.start, hf * HALF + cols.stop)
                last = mm(PJ[:, g % 2, cols], wsl[:, w % NSLOT, a, k], actT[:, b, k, c],
                          start=(r == 0), stop=(r == 3 * KD - 1))
                if r == 3 * KD - 1 and cols.stop == HALF:
                    last.then_inc(s["proj_done"], 1)

            def sum_squares(it, n, extra=0):
                pe.wait_ge(s["sql_done"], it * 6 + (n + 1))
                pe.wait_ge(s["ss_read"], it * 8 + (TURN[n] + 2 + extra))
                mm(SS[:, :], ones[:, :], sqh[:, n % 2], start=True, stop=False)
                mm(SS[:, :], ones[:, :], sql[:, n % 2], start=False, stop=True).then_inc(s["ones_done"], 1)

            def score(it, u):
                t, hh = u // 2, u % 2
                nb = keys(u)
                hp = slice(hh * HD, (hh + 1) * HD)
                if u in (0, 8):
                    pe.wait_ge(s["qklo_done"], it * 4 + (2 if u == 0 else 4))
                if u:
                    pe.wait_ge(s["sm_done"], it * UNITS + u)
                at = score_at(u)
                k0 = (t - nb + 1) * P - at
                for c0, c1 in ((at, min(HALF, at + nb * P)), (HALF, at + nb * P)):
                    if c0 < c1:
                        for n, (a, b) in enumerate(PASSES):
                            last = mm(SC[:, c0:c1], qT[hp, a, t * P:(t + 1) * P], kT[hp, b, k0 + c0:k0 + c1],
                                      start=(n == 0), stop=(n == 2))
                last.then_inc(s["sc_done"], 1)

            def prob_transpose(it, u):
                pe.wait_ge(s["exp_done"], it * UNITS + (u + 1))
                if u == 8:
                    pe.wait_ge(s["vlo_done"], it * 2 + 2)
                if u:
                    pe.wait_ge(s["ptlo_done"], it * UNITS + u)
                for j in range(keys(u)):
                    last = nc.tensor.transpose(PT[:, j * P:(j + 1) * P], prob[:, u % 2, j * P:(j + 1) * P], ident[:, :])
                last.then_inc(s["pt_done"], 1)

            def prob_v(it, u):
                t, hh = u // 2, u % 2
                nb = keys(u)
                pe.wait_ge(s["ptlo_done"], it * UNITS + (u + 1))
                if u == 0:
                    pe.wait_ge(s["vlo_done"], it * 2 + 1)
                if u % 2 == 0 and u:
                    pe.wait_ge(s["oq_done"], it * (UNITS // 2) + u // 2)
                for j in range(nb):
                    last = mm(UP,
                              V[:, t - nb + 1 + j, hh].rearrange("p a d -> p (a d)"), pT[:, :, j * P:(j + 1) * P],
                              start=(j == 0), stop=(j == nb - 1))
                last.then_inc(s["pv_done"], 1)

            def u_transpose(it, u):
                pe.wait_ge(s["us_done"], it * UNITS + (u + 1))
                nc.tensor.transpose(UQ[:, u % 2 * P:(u % 2 + 1) * P], uT[:, u % 2], ident[:, :]).then_inc(s["uq_done"], 1)

            def o_transpose(it, g, turn):
                pe.wait_ge(s["on_done"], it * 2 + (g + 1))
                pe.wait_ge(s["ss_read"], it * 8 + (turn + 2))
                for t in range(4):
                    last = nc.tensor.transpose(SS[:, t * P:(t + 1) * P], on[:, g, t * P:(t + 1) * P], ident[:, :])
                last.then_inc(s["ot_done"], 1)

            def w_out_products(t, hf, k):
                for n, (a, b) in enumerate(PASSES):
                    last = mm(SC[:, half(hf)] if t == 1 else PJ[:, hf], actT[:, a, k, col(t)], wo[:, k, b, half(hf)],
                              start=(k == 0 and n == 0), stop=(k == KD - 1 and n == 2))
                if k == KD - 1:
                    last.then_inc(s["mm2_done" if t == NT - 1 and hf else "proj_done"], 1)

            def w_out_both(k, tiles=(0, 1)):
                for t in tiles:
                    if k == 0:
                        pe.wait_ge(s["ym_ready"], t + 1)
                    if t == 0:
                        mine, sem = (POOL_WO, "woq_ready") if k in POOL_WO else (VEC_WO, "wo_ready")
                        pe.wait_ge(s[sem], mine.index(k) + 1)
                    for hf in range(2):
                        w_out_products(t, hf, k)

            def v_transpose(it, n):
                pe.wait_ge(s["vcopy_done"], it * 2 + (n + 1))
                for t in range(4):
                    last = nc.tensor.transpose(PT[:, HALF + t * P:HALF + (t + 1) * P], vT[:, t * P:(t + 1) * P], ident[:, :])
                last.then_inc(s["vt_done"], 1)

            def iteration(it, last):
                n = 0

                def fill(count):
                    nonlocal n
                    for m in range(n, n + count):
                        g = NLEAD + m // (3 * KD)
                        group_product(it + g // G, g % G, m % (3 * KD))
                    n += count

                def extras(at):
                    if at == "1a":
                        sum_squares(it, 2)
                    if at == "4a":
                        sum_squares(it, 3)
                    if at == "4b":
                        v_transpose(it, 1)
                    if at == "10b":
                        sum_squares(it, 4)
                    if at == "12a":
                        o_transpose(it, 0, OTURN[0])
                    if at == "14b" and not last:
                        sum_squares(it, 5)
                    if at == "15b" and not last:
                        sum_squares(it + 1, 0)
                    if last:
                        if at == "15a":
                            w_out_both(0, (0,))
                        if at == "15b":
                            w_out_both(0, (1,))
                            w_out_both(1, (0,))

                score(it, 0)
                fill(4)
                for u in range(UNITS):
                    count = (FILL_LAST if last else FILL)[u] - (4 if u == 0 else 0)
                    if u >= 2:
                        u_transpose(it, u - 2)
                    if u + 1 < UNITS:
                        score(it, u + 1)
                    fill(count // 2)
                    extras(f"{u}a")
                    if u >= 1:
                        prob_v(it, u - 1)
                    prob_transpose(it, u)
                    fill(count - count // 2)
                    extras(f"{u}b")
                if not last:
                    rest = REST + 4 * 3 * KD - n
                    fill(rest - 54)
                    u_transpose(it, UNITS - 2)
                    prob_v(it, UNITS - 1)
                    fill(8)
                    u_transpose(it, UNITS - 1)
                    fill(10)
                    sum_squares(it + 1, 1)
                    fill(18)
                    v_transpose(it + 1, 0)
                    fill(18)
                    o_transpose(it, 1, OTURN[1])
                else:
                    assert n == REST
                    u_transpose(it, UNITS - 2)
                    prob_v(it, UNITS - 1)
                    sum_squares(it, 5)
                    w_out_both(1, (1,))
                    u_transpose(it, UNITS - 1)
                    for k in range(2, KD):
                        w_out_both(k)
                        if k == 4:
                            o_transpose(it, 1, LAST_OTURN)

            for t in range(3):
                x_transpose(t)
            pe.wait_ge(s["xlo_done"], 2)
            for r in range(3 * KD):
                if r == 18:
                    x_transpose(3)
                group_product(0, 0, r, first=True, cols=slice(0, HALF // 2))
            pe.wait_ge(s["xlo_done"], 4)
            for r in range(3 * KD):
                if r == 12:
                    x_transpose(4)
                group_product(0, 0, r, first=True, cols=slice(HALF // 2, HALF))
            pe.wait_ge(s["mask_set"], 3)
            for g in (1,):
                for r in range(3 * KD):
                    if r in (4, 12, 20):
                        x_transpose(5 + r // 8)
                    group_product(0, g, r, first=True)
                if g:
                    sum_squares(0, 0, 1)
            for r in range(3 * KD):
                group_product(0, 2, r)
            sum_squares(0, 1, 1)
            pe.wait_ge(s["xlo_done"], NT)
            for r in range(3 * KD):
                group_product(0, 3, r)
                if r == 10:
                    v_transpose(0, 0)
            with pe.Fori(0, NPAIR - 1) as it:
                iteration(it, False)
            iteration(NPAIR - 1, True)

            def h_transpose(t):
                pe.wait_ge(s["xs_done"], NT + t + 1)
                if t >= 2:
                    pe.wait_ge(s["xlo_done"], NT + t - 1)
                bank = (PT, SC)[t % 2]
                for k in range(KD):
                    last = nc.tensor.transpose(bank[:, k * P:(k + 1) * P], ymix[:, t, k, :], ident[:, :])
                last.then_inc(s["tr_done"], 1)

            for t in range(2, NT):
                pe.wait_ge(s["ym_ready"], t + 1)
                for hf in range(2):
                    pe.wait_ge(s["hadd_done"], 2 * t - 1 + hf if t > 2 else 1 + hf)
                    for k in range(KD):
                        w_out_products(t, hf, k)
                    if t == 2 and hf == 0:
                        h_transpose(0)
                h_transpose(t - 1)
            def mm1(b, g, r0=0, r1=3 * KD):
                f = g // 2
                if r0 == 0:
                    if g % 2 == 0:
                        pe.wait_ge(s["w_ready"], b * ND + (N_B + D_ORDER.index(("w1", f)) + 1))
                    if g >= 2:
                        pe.wait_ge(s["hsq_done"], b * (2 * FT) + (g - 1))
                for r in range(r0, r1):
                    k, (x0, x1) = r // 3, PASSES[r % 3]
                    last = mm(PJ[:, g % 2], w1[:, f % 2, x0, k], actT[:, x1, k, half(1 - g % 2)],
                              start=(r == 0), stop=(r == 3 * KD - 1))
                if r1 == 3 * KD:
                    last.then_inc(s["mm1_done"], 1)

            def mm2(t, a, f):
                for n, (x0, x1) in enumerate(PASSES):
                    last = mm(MM2BANK[2 * (t % 3) + a], hid[:, x0, f, col(t)], w2[:, x1, f, half(a)],
                              start=(f == 0 and n == 0), stop=(f == FT - 1 and n == 2))
                if f == FT - 1:
                    last.then_inc(s["mm2_done"], 1)

            def mlp_block(b):
                for g in range(1, 2 * FT):
                    mm1(b, g)
                pe.wait_ge(s["w_ready"], b * ND + (N_B + ND))
                for fs in (range(FT - 1), range(FT - 1, FT)):
                    pe.wait_ge(s["hlo_done"], b * (2 * FT) + (2 * fs[-1] + 1))
                    for t in range(2):
                        for a in range(2):
                            for f in fs:
                                mm2(t, a, f)
                pe.wait_ge(s["hlo_done"], b * (2 * FT) + 2 * FT)
                for t in range(2, NT):
                    for a in range(2):
                        if t >= 3:
                            pe.wait_ge(s["acc_done"], b * (2 * NT) + (2 * (t - 3) + a + 1))
                        for f in range(FT):
                            mm2(t, a, f)

            pe.wait_ge(s["xlo_done"], NT + NT // 2)
            pe.wait_ge(s["hadd_done"], 2 * NT - 1)
            mm1(0, 0, 0, 15)
            h_transpose(NT - 1)
            mm1(0, 0, 15, 3 * KD)
            pe.wait_ge(s["hadd_done"], 2 * NT)
            pe.wait_ge(s["xlo_done"], 2 * NT)
            with pe.Fori(0, NFB - 1) as b:
                mlp_block(b)
                mm1(b + 1, 0)
            mlp_block(NFB - 1)


_INS = ["x", "norm_mix_g", "w_in", "conv_w", "conv_b", "q_norm_g", "k_norm_g", "rel_bias",
        "conv_out_g", "attn_out_g", "w_out", "norm_mlp_g", "w_mlp_in", "w_mlp_out"]


def kernel(**inputs):
    import numpy as np
    import concourse.bacc as bacc
    from concourse.bass_utils import run_bass_kernel_spmd

    nc = bacc.Bacc("TRN2", target_bir_lowering=False, num_devices=1)
    arrays, args = {}, []
    for name in _INS:
        a = np.ascontiguousarray(inputs[name])
        arrays[f"in_{name}"] = a
        args.append(nc.dram_tensor(f"in_{name}", a.shape, mybir.dt.from_np(a.dtype), kind="ExternalInput").ap())
    args.append(nc.dram_tensor("out_0", (1, SEQ, DM), F32, kind="ExternalOutput").ap())
    build(nc, *args)
    r = run_bass_kernel_spmd(nc, [arrays], core_ids=[0])
    return r.results[0]["out_0"]
```
